# Optimizing a Trainium2 kernel written in Bass

```python
import math
import jax, jax.numpy as jnp
from jax import lax
import numpy as np

'''One inference step of a hybrid diffusion / flow-matching backbone (DEPTH layers).

Each layer: adaLN modulation -> three parallel token mixers (bidirectional HGRN2 gated linear
recurrence, FNet-style 2-D Fourier mixing per channel group, short gated width-3 convolution)
sharing one combined input projection -> per-branch projections to D_MODEL -> per-channel sigmoid
branch gates -> one output projection -> DeepNorm post-LayerNorm; then adaLN-modulated fine-grained
sigmoid-routed top-k MoE with one shared expert -> DeepNorm post-LayerNorm.

Inputs:
  x_prompt   (BATCH, SEQ, D_MODEL)          context tokens of new requests (group i)
  x_sample   (DEC_BATCH, DEC_SEQ, D_MODEL)  noisy latent tokens on a GRID_W-wide grid (group ii)
  c          (DEC_BATCH, D_MODEL)           conditioning vector of each denoising request
  state_hgrn (DEC_BATCH, DEPTH, 2, HGRN_HEADS, HGRN_HEAD_DIM, HGRN_HEAD_DIM)
             cached final context-scan states (direction 0 = forward, 1 = backward) of PAST_LEN
             context tokens
  c_ctx      (D_MODEL,)                     learned constant modulation vector for context tokens
  weights    stacked over a leading DEPTH axis
Returns the tuple (y_prompt, y_sample, state_hgrn_new):
  y_prompt       (BATCH, SEQ, D_MODEL)
  y_sample       (DEC_BATCH, DEC_SEQ, D_MODEL)
  state_hgrn_new (BATCH, DEPTH, 2, HGRN_HEADS, HGRN_HEAD_DIM, HGRN_HEAD_DIM)
'''

D_MODEL = 1024
BATCH = 1
SEQ = 128
DEPTH = 1
DEC_BATCH = 1
DEC_SEQ = 128
PAST_LEN = 128

GRID_W = 64
HGRN_HEADS = 4
HGRN_HEAD_DIM = 128
HGRN_WIDTH = HGRN_HEADS * HGRN_HEAD_DIM
HGRN_CHUNK = 64
FOURIER_GROUPS = 4
FOURIER_GROUP_DIM = 64
FOURIER_WIDTH = FOURIER_GROUPS * FOURIER_GROUP_DIM
CONV_GROUPS = 4
CONV_WIDTH = 256
CONV_K = 3
N_BRANCHES = 3
IN_SPLITS = (HGRN_WIDTH, HGRN_WIDTH, HGRN_WIDTH, HGRN_WIDTH, HGRN_WIDTH, FOURIER_WIDTH, CONV_WIDTH, CONV_WIDTH, CONV_WIDTH, N_BRANCHES * D_MODEL)
IN_COLS = sum(IN_SPLITS)
N_EXPERTS = 64
TOP_K = 8
D_EXPERT = 256
D_SHARED = 256
ROUTED_SCALE = 2.5
ALPHA = (2 * DEPTH) ** 0.25
BETA = (8 * DEPTH) ** -0.25
LN_EPS = 1e-6
RMS_EPS = 1e-6
F_MIN = 1e-30

kernel_name = 'hybrid_hgrn2_fnet_conv_moe_diffusion_step'

F32 = jnp.float32

def _layer_norm(x, gain=None, bias=None):
    xf = x.astype(F32)
    xc = xf - jnp.mean(xf, axis=-1, keepdims=True)
    y = xc * lax.rsqrt(jnp.mean(xc * xc, axis=-1, keepdims=True) + LN_EPS)
    if gain is not None:
        y = y * gain + bias
    return y.astype(x.dtype)

def _grid_pos_emb(rows, dtype):
    t = jnp.arange(rows * GRID_W)
    r = (t // GRID_W).astype(F32)
    col = (t % GRID_W).astype(F32)
    quarter = D_MODEL // 4
    omega = 1.0 / (10000.0 ** (jnp.arange(quarter, dtype=F32) / quarter))
    ar = r[:, None] * omega
    ac = col[:, None] * omega
    return jnp.concatenate([jnp.sin(ar), jnp.cos(ar), jnp.sin(ac), jnp.cos(ac)], axis=-1).astype(dtype)

def _gated_chunk_scan(q, k, v, log_f, s0):
    bsz, nh, T, _ = q.shape
    dv = v.shape[-1]
    n_chunks = T // HGRN_CHUNK

    def to_chunks(a):
        a = a.reshape(bsz, nh, n_chunks, HGRN_CHUNK, a.shape[-1])
        return jnp.moveaxis(a, 2, 0)

    causal = jnp.tril(jnp.ones((HGRN_CHUNK, HGRN_CHUNK), dtype=bool))[:, :, None]

    def step(S, chunk):
        qc, kc, vc, lfc = chunk
        b = jnp.cumsum(lfc, axis=2)
        diff = jnp.where(causal, b[:, :, :, None, :] - b[:, :, None, :, :], 0.0)
        decay = jnp.where(causal, jnp.exp(diff), 0.0)
        scores = jnp.einsum('bhtd,bhtsd->bhts', qc, decay * kc[:, :, None, :, :])
        o = jnp.einsum('bhts,bhsv->bhtv', scores, vc) + jnp.einsum('bhtd,bhdv->bhtv', qc * jnp.exp(b), S)
        g = b[:, :, -1:, :]
        S = jnp.exp(g[:, :, 0, :, None]) * S + jnp.einsum('bhsd,bhsv->bhdv', kc * jnp.exp(g - b), vc)
        return S, o

    s_final, o = lax.scan(step, s0, (to_chunks(q), to_chunks(k), to_chunks(v), to_chunks(log_f)))
    o = jnp.moveaxis(o, 0, 2).reshape(bsz, nh, T, dv)
    return o, s_final

def _hgrn2_branch(u_q, u_i, u_f_fwd, u_f_bwd, u_g, lb, norm_g, s0):
    bsz, T, _ = u_q.shape

    def heads(a):
        return a.astype(F32).reshape(bsz, T, HGRN_HEADS, HGRN_HEAD_DIM).transpose(0, 2, 1, 3)

    def flip(a):
        return a[:, :, ::-1]

    q = heads(jax.nn.silu(u_q.astype(F32)))
    v = heads(u_i)
    s0 = s0.astype(F32)
    outs = []
    finals = []
    for d, u_f in enumerate((u_f_fwd, u_f_bwd)):
        z = u_f.astype(F32)
        lbd = lb[d]
        f = lbd + (1.0 - lbd) * jax.nn.sigmoid(z)
        log_f = jnp.log(jnp.maximum(f, F_MIN))
        k = (1.0 - lbd) * jax.nn.sigmoid(-z)
        qd, kd, vd, lfd = q, heads(k), v, heads(log_f)
        if d == 1:
            qd, kd, vd, lfd = flip(qd), flip(kd), flip(vd), flip(lfd)
        o, s_fin = _gated_chunk_scan(qd, kd, vd, lfd, s0[:, d])
        if d == 1:
            o = flip(o)
        outs.append(o)
        finals.append(s_fin)
    o = (outs[0] + outs[1]).transpose(0, 2, 1, 3)
    o = o * lax.rsqrt(jnp.mean(o * o, axis=-1, keepdims=True) + RMS_EPS)
    o = o.reshape(bsz, T, HGRN_WIDTH) * norm_g * jax.nn.silu(u_g.astype(F32))
    return o.astype(u_q.dtype), jnp.stack(finals, axis=1)

def _fourier_branch(u):
    bsz, T, _ = u.shape
    z = u.astype(F32).reshape(bsz, T, FOURIER_GROUPS, FOURIER_GROUP_DIM)
    z = jnp.fft.fft2(z, axes=(1, 3), norm='ortho').real
    return z.reshape(bsz, T, FOURIER_WIDTH).astype(u.dtype)

def _short_conv_branch(u_b, u_c, u_h, conv_w):
    z = u_c * u_h
    zp = jnp.pad(z, ((0, 0), (1, 1), (0, 0)))
    y = conv_w[0] * zp[:, :-2] + conv_w[1] * zp[:, 1:-1] + conv_w[2] * zp[:, 2:]
    return u_b * y

def _moe(h, w_router, b_router, w_exp_gate, w_exp_up, w_exp_down, w_sh_gate, w_sh_up, w_sh_down):
    scores = jax.nn.sigmoid(jnp.einsum('btd,de->bte', h.astype(F32), w_router.astype(F32)))
    _, idx = lax.top_k(scores + b_router.astype(F32), TOP_K)
    sel = jnp.take_along_axis(scores, idx, axis=-1)
    wts = ROUTED_SCALE * sel / (jnp.sum(sel, axis=-1, keepdims=True) + 1e-20)
    gate = jnp.sum(jax.nn.one_hot(idx, N_EXPERTS, dtype=F32) * wts[..., None], axis=-2).astype(h.dtype)
    hid = jax.nn.silu(jnp.einsum('btd,edf->btef', h, w_exp_gate)) * jnp.einsum('btd,edf->btef', h, w_exp_up)
    routed = jnp.einsum('btef,efd->btd', hid * gate[..., None], w_exp_down)
    shared = (jax.nn.silu(h @ w_sh_gate) * (h @ w_sh_up)) @ w_sh_down
    return routed + shared

def _trunk_layer(x, cond, s0, lb, w_ada, b_ada, w_in, b_gate, hgrn_norm, conv_w, w_proj_hgrn, w_proj_fourier,
                 w_proj_conv, w_out, ln1_g, ln1_b, ln2_g, ln2_b, w_router, b_router, w_exp_gate, w_exp_up,
                 w_exp_down, w_sh_gate, w_sh_up, w_sh_down):
    bsz, T, _ = x.shape
    mod = jax.nn.silu(cond) @ w_ada + b_ada
    sh1, sc1, g1, sh2, sc2, g2 = [m[:, None, :] for m in jnp.split(mod, 6, axis=-1)]
    h = _layer_norm(x) * (1.0 + sc1) + sh1
    u = h @ w_in
    uq, ui, uff, ufb, ug, ufour, ucb, ucc, uch, ugate = jnp.split(u, np.cumsum(IN_SPLITS)[:-1], axis=-1)
    a, s_final = _hgrn2_branch(uq, ui, uff, ufb, ug, lb, hgrn_norm, s0)
    f = _fourier_branch(ufour)
    cv = _short_conv_branch(ucb, ucc, uch, conv_w)
    gates = jax.nn.sigmoid(ugate + b_gate).reshape(bsz, T, N_BRANCHES, D_MODEL)
    merged = (gates[:, :, 0] * (a @ w_proj_hgrn) + gates[:, :, 1] * (f @ w_proj_fourier)
              + gates[:, :, 2] * (cv @ w_proj_conv))
    x = _layer_norm(ALPHA * x + g1 * (merged @ w_out), ln1_g, ln1_b)
    h = _layer_norm(x) * (1.0 + sc2) + sh2
    ffn = _moe(h, w_router, b_router, w_exp_gate, w_exp_up, w_exp_down, w_sh_gate, w_sh_up, w_sh_down)
    x = _layer_norm(ALPHA * x + g2 * ffn, ln2_g, ln2_b)
    return x, s_final

def setup_inputs(seed: int = 0) -> dict:
    key = jax.random.key(seed)
    ks = iter(jax.random.split(key, 32))

    def nrm(shape, scale):
        return scale * jax.random.normal(next(ks), shape, F32)

    D = D_MODEL
    return {
        'x_prompt': nrm((BATCH, SEQ, D), 1.0),
        'x_sample': nrm((DEC_BATCH, DEC_SEQ, D), 1.0),
        'c': nrm((DEC_BATCH, D), 1.0),
        'state_hgrn': nrm((DEC_BATCH, DEPTH, 2, HGRN_HEADS, HGRN_HEAD_DIM, HGRN_HEAD_DIM), 0.5),
        'c_ctx': nrm((D,), 1.0),
        'w_ada': nrm((DEPTH, D, 6 * D), D ** -0.5),
        'b_ada': nrm((DEPTH, 6 * D), 0.02),
        'w_in': nrm((DEPTH, D, IN_COLS), D ** -0.5),
        'b_gate': nrm((DEPTH, N_BRANCHES * D), 0.02),
        'hgrn_lb': nrm((DEPTH, 2, HGRN_WIDTH), 1.0),
        'hgrn_norm': 1.0 + nrm((DEPTH, HGRN_WIDTH), 0.02),
        'conv_w': nrm((DEPTH, CONV_K, CONV_WIDTH), CONV_K ** -0.5),
        'w_proj_hgrn': nrm((DEPTH, HGRN_WIDTH, D), HGRN_WIDTH ** -0.5),
        'w_proj_fourier': nrm((DEPTH, FOURIER_WIDTH, D), FOURIER_WIDTH ** -0.5),
        'w_proj_conv': nrm((DEPTH, CONV_WIDTH, D), CONV_WIDTH ** -0.5),
        'w_out': nrm((DEPTH, D, D), BETA * D ** -0.5),
        'ln1_g': 1.0 + nrm((DEPTH, D), 0.02),
        'ln1_b': nrm((DEPTH, D), 0.02),
        'ln2_g': 1.0 + nrm((DEPTH, D), 0.02),
        'ln2_b': nrm((DEPTH, D), 0.02),
        'w_router': nrm((DEPTH, D, N_EXPERTS), D ** -0.5),
        'b_router': nrm((DEPTH, N_EXPERTS), 0.01),
        'w_exp_gate': nrm((DEPTH, N_EXPERTS, D, D_EXPERT), D ** -0.5),
        'w_exp_up': nrm((DEPTH, N_EXPERTS, D, D_EXPERT), D ** -0.5),
        'w_exp_down': nrm((DEPTH, N_EXPERTS, D_EXPERT, D), BETA * D_EXPERT ** -0.5),
        'w_sh_gate': nrm((DEPTH, D, D_SHARED), D ** -0.5),
        'w_sh_up': nrm((DEPTH, D, D_SHARED), D ** -0.5),
        'w_sh_down': nrm((DEPTH, D_SHARED, D), BETA * D_SHARED ** -0.5),
    }

def reference(x_prompt, x_sample, c, state_hgrn, c_ctx, w_ada, b_ada, w_in, b_gate, hgrn_lb, hgrn_norm, conv_w,
              w_proj_hgrn, w_proj_fourier, w_proj_conv, w_out, ln1_g, ln1_b, ln2_g, ln2_b, w_router, b_router,
              w_exp_gate, w_exp_up, w_exp_down, w_sh_gate, w_sh_up, w_sh_down):
    lb_sm = jax.nn.softmax(hgrn_lb.astype(F32), axis=0)
    lb_all = jnp.cumsum(lb_sm, axis=0) - lb_sm[:1]
    rows = x_sample.shape[1] // GRID_W
    xc = x_prompt
    xs = x_sample + _grid_pos_emb(rows, x_sample.dtype)[None]
    zero_state = jnp.zeros((x_prompt.shape[0], 2, HGRN_HEADS, HGRN_HEAD_DIM, HGRN_HEAD_DIM), F32)
    ctx_cond = c_ctx[None, :]
    new_states = []
    for l in range(DEPTH):
        lw = (w_ada[l], b_ada[l], w_in[l], b_gate[l], hgrn_norm[l], conv_w[l], w_proj_hgrn[l],
              w_proj_fourier[l], w_proj_conv[l], w_out[l], ln1_g[l], ln1_b[l], ln2_g[l], ln2_b[l],
              w_router[l], b_router[l], w_exp_gate[l], w_exp_up[l], w_exp_down[l], w_sh_gate[l],
              w_sh_up[l], w_sh_down[l])
        xc, s_ctx = _trunk_layer(xc, ctx_cond, zero_state, lb_all[l], *lw)
        new_states.append(s_ctx)
        xs, _ = _trunk_layer(xs, c, state_hgrn[:, l], lb_all[l], *lw)
    state_hgrn_new = jnp.stack(new_states, axis=1)
    return (xc, xs, state_hgrn_new)


_drawn_inputs = setup_inputs


def setup_inputs(seed=0):
    import zlib

    import numpy as np

    out = dict(_drawn_inputs(seed))
    spreads = {}
    factors = {'state_hgrn': 8.0, 'b_gate': 3.844, 'hgrn_norm': 2.837, 'ln2_g': 2.9, 'ln2_b': 2.841}
    for name, (base, spread) in spreads.items():
        noise = np.random.default_rng([zlib.crc32(name.encode()), seed]).standard_normal(out[name].shape)
        drawn = base * np.exp(spread * noise) if base else spread * noise
        out[name] = __import__('jax').numpy.asarray(drawn.astype(out[name].dtype))
    for name, factor in factors.items():
        out[name] = (out[name] * factor).astype(out[name].dtype)
    return out
```

```python
from contextlib import ExitStack

import numpy as np

import concourse.bass as bass
from concourse import mybir
from concourse.alu_op_type import AluOpType as ALU

F32 = mybir.dt.float32
F32R = mybir.dt.float32r
I32 = mybir.dt.int32
U8 = mybir.dt.uint8
ACT = mybir.ActivationFunctionType
AXX = mybir.AxisListType.X

P = 128
D = 1024
KD = D // P
G = 2
TOK = G * P
HEADS, DK = 4, 128
HW = HEADS * DK
FGD = 64
FW = 256
CW = 256
NB = 3
N_EXP, TOP_K, DE = 64, 8, 256
ROUTED_SCALE = 2.5
ALPHA = 2 ** 0.25
LN_EPS = 1e-6
RMS_EPS = 1e-6
F_MIN = 1e-30
LN_SPLIT = 2.0 ** -60
BANK = 512

LEVELS = [64, 32, 16, 8, 4, 2, 1]
N_MASK = 2 * len(LEVELS) + 1
SLOTS = 64
MAX_CHUNKS = TOK // SLOTS
MAX_ITEMS = 96
ITEMS_PER_TURN = 4

CST_COLS = {}


def shape_constants():
    parts = []

    def put(name, a):
        at = sum(x.shape[1] for x in parts)
        CST_COLS[name] = (at, at + a.shape[1])
        full = np.zeros((P, a.shape[1]), np.float32)
        full[:a.shape[0]] = a
        parts.append(full)

    i = np.arange(P)
    put("ident", np.eye(P))
    put("ones", np.ones((P, P)))
    put("before", (i[:, None] < i[None, :]))
    put("slot_no", np.tile(np.arange(SLOTS) + 1.0, 2)[None].repeat(P, 0))
    put("item_no", np.arange(MAX_ITEMS)[None].repeat(P, 0))
    put("chunk_no", np.arange(MAX_CHUNKS)[None].repeat(P, 0))
    put("chunk_at", (np.arange(MAX_CHUNKS) * SLOTS)[None].repeat(P, 0))
    put("part_no", i[:, None])
    keep = sum(x.shape[1] for x in parts)
    scale = 1.0 / np.sqrt(P * FGD)
    angle = 2 * np.pi * ((i[:, None] * i[None, :]) % P) / P
    put("dft_t", np.concatenate([np.cos(angle), np.sin(angle)], 1) * scale)
    c = np.arange(FGD)
    angle = 2 * np.pi * ((c[:, None] * c[None, :]) % FGD) / FGD
    put("dft_c", np.concatenate([np.kron(np.eye(P // FGD), np.cos(angle)),
                                 np.kron(np.eye(P // FGD), -np.sin(angle))], 1))
    table = np.concatenate(parts, 1).astype(np.float32)

    masks = np.zeros((P, N_MASK, P), np.float32)
    for direction in range(2):
        for n, half in enumerate(LEVELS):
            same = (i[:, None] // (2 * half)) == (i[None, :] // (2 * half))
            s_late = (i[:, None] // half) % 2 == 1
            t_late = (i[None, :] // half) % 2 == 1
            pick = same & ~s_late & t_late if direction == 0 else same & s_late & ~t_late
            masks[:, direction * len(LEVELS) + n] = pick
    masks[:, -1] = np.eye(P)

    quarter = D // 4
    omega = (1.0 / (10000.0 ** (np.arange(quarter, dtype=np.float32) / np.float32(quarter)))).astype(np.float32)
    row, col = (i // 64).astype(np.float32), (i % 64).astype(np.float32)
    ar, ac = row[:, None] * omega, col[:, None] * omega
    pos = np.concatenate([np.sin(ar), np.cos(ar), np.sin(ac), np.cos(ac)], -1).astype(np.float32)
    return table, keep, masks.reshape(P, N_MASK * P), pos


CST, CST_KEEP, MASKS, POS = shape_constants()

RING = 3
CH_BYTES = KD * BANK
ADA_EARLY = [0, 1, 2, 3, 4, 5]
ADA_LATE = [6, 7, 8, 9, 10, 11]
IN_ORDER = [2, 3, 0, 1, 4, 5, 6, 7, 8, 9, 10, 11, 12]
CHUNKS = ([("ada", c) for c in ADA_EARLY] + [("in", c) for c in IN_ORDER]
          + [("ada", c) for c in ADA_LATE]
          + [("proj_hgrn", 0), ("proj_fc", 0), ("out", 0), ("out", 1), ("shared_up", 0), ("shared_down", 0)])
CHUNK_NO = {c: n for n, c in enumerate(CHUNKS)}
CHUNK_DMAS = {"ada": 1, "in": 1, "proj_hgrn": 1, "proj_fc": 2, "out": 1, "shared_up": 2, "shared_down": 1}


def chunk_arrived(chunk):
    n = CHUNK_NO[chunk]
    return n % RING, 16 * sum(CHUNK_DMAS[CHUNKS[m][0]] for m in range(n % RING, n + 1, RING))


RAW = 2 * RING


def raw_slot(p):
    return (p[1] + 2) % RAW


PRODUCTS = ([("ada", c) for c in ADA_EARLY]
            + [("in", c, h) for c in IN_ORDER for h in range(2)]
            + [("ada", c) for c in ADA_LATE]
            + [("proj", g, h, b) for g in range(G) for h in range(2) for b in range(NB)]
            + [("out", h, g) for h in range(2) for g in range(G)]
            + [("shared", f) for f in range(2)])
PRODUCT_NO = {p: n for n, p in enumerate(PRODUCTS)}
N_ROT = 3

class Count:

    def __init__(self, register, scale, more):
        self.register, self.scale, self.more = register, scale, more

    def __add__(self, k):
        return Count(self.register, self.scale, self.more + k)

    def __sub__(self, k):
        return self + -k

    def __mul__(self, k):
        return Count(self.register, k * self.scale, k * self.more)

    __rmul__ = __mul__

    def value(self):
        assert self.more >= 0
        return self.register * self.scale + self.more if self.more else self.register * self.scale


def val(n):
    return n.value() if isinstance(n, Count) else n


def above_zero(n):
    return isinstance(n, Count) or n > 0


STEPS = [(d, g, n) for d in range(2) for g in range(G) for n in range(len(LEVELS))] + \
        [(None, g, None) for g in range(G)]
SCRATCH = ([("h", g, a) for g in range(G) for a in range(2)]
           + [("step", s) for s in range(len(STEPS))]
           + [("four1", g) for g in range(G)]
           + [("ends", d) for d in range(2)] + [("state", d) for d in range(2)]
           + [("four2",)] + [("a", g) for g in range(G)]
           + [("merged", g, a) for g in range(G) for a in range(2)]
           + [("h2", g, a) for g in range(G) for a in range(2)]
           + [("logits",), ("place",), ("count",), ("before",), ("rows",), ("items",), ("item_rows",)])
SCRATCH_NO = {u: n for n, u in enumerate(SCRATCH)}
STEP_FROM = PRODUCT_NO[("in", 4, 0)]


def schedule():
    left = list(range(len(STEPS)))
    for n in range(PRODUCT_NO[("in", IN_ORDER[0], 0)], PRODUCT_NO[("ada", ADA_LATE[-1])] + 1):
        yield "product", PRODUCTS[n]
        if n >= STEP_FROM:
            for s in left[:2]:
                yield "step", s
            left = left[2:]
    for s in left:
        yield "step", s


def hybrid_layer(nc, x_prompt, x_sample, c, state_hgrn, c_ctx, w_ada, b_ada, w_in, b_gate, hgrn_lb, hgrn_norm,
                 conv_w, w_proj_hgrn, w_proj_fourier, w_proj_conv, w_out, ln1_g, ln1_b, ln2_g, ln2_b, w_router,
                 b_router, w_exp_gate, w_exp_up, w_exp_down, w_sh_gate, w_sh_up, w_sh_down,
                 table, masks, pos, y_prompt, y_sample, state_new):
    ctx = ExitStack()
    with ctx:
        def sem(name):
            return ctx.enter_context(nc.semaphore(name))

        mixer_sbuf, experts_sbuf = ExitStack(), ExitStack()

        def keep(name, shape, dt=F32):
            return ctx.enter_context(nc.sbuf_tensor(name, shape, dt))

        def mix(name, shape, dt=F32):
            return mixer_sbuf.enter_context(nc.sbuf_tensor(name, shape, dt))

        def moe(name, shape, dt=F32):
            return experts_sbuf.enter_context(nc.sbuf_tensor(name, shape, dt))

        ring = keep("ring", [P, RING, CH_BYTES])
        cst = keep("cst", [P, CST_KEEP])
        resid = keep("resid", [P, G, D])
        gate2 = keep("gate2", [P, G, D])
        bn = keep("bn", [P, 2, 6])
        mv = keep("mv", [P, 2])
        vareps = keep("vareps", [P, 1])
        std = keep("std", [P, 1])
        rstd = keep("rstd", [P, 1])
        counts = keep("counts", [P, 1])
        has_chunk = keep("has_chunk", [P, MAX_CHUNKS])
        n_chunks = keep("n_chunks", [P, 1])
        item_expert = keep("item_expert", [1, MAX_ITEMS], I32)
        last_turn = keep("last_turn", [1, 2], I32)

        def con(name):
            a, b = CST_COLS[name]
            return cst[:, a:b]

        ident, ones, before = con("ident"), con("ones"), con("before")

        dft = mix("dft", [P, table.shape[1] - CST_KEEP])
        mask_sb = mix("mask_sb", [P, N_MASK, P], U8)
        cond_t = mix("cond_t", [P, G, KD])
        cond_s = mix("cond_s", [P, KD, G])
        mod_row = mix("mod_row", [G, 2, BANK])
        b_ada_sb = mix("b_ada_sb", [G, 2, BANK])
        mod_a = mix("mod_a", [P, G, D])
        mod_b = mix("mod_b", [P, G, D])
        h_t = mix("h_t", [P, KD, TOK])
        gates = mix("gates", [P, G, NB, D])
        fgate = mix("fgate", [P, 2, HEADS, TOK])
        kgate = mix("kgate", [P, 2, HEADS, TOK])
        decay = mix("decay", [P, 2, HEADS, TOK])
        q_t = mix("q_t", [P, HEADS, TOK])
        tmp = mix("tmp", [P, HEADS, TOK])
        lb_in = mix("lb_in", [P, 2 * HEADS])
        lb = mix("lb", [P, 2 * HEADS])
        lb_e = mix("lb_e", [P, 2 * HEADS])
        lb_one = mix("lb_one", [P, 2 * HEADS])
        value = mix("value", [P, G, HW])
        out_gate = mix("out_gate", [P, G, HW])
        norm_row = mix("norm_row", [P, HW])
        four = mix("four", [P, G, FW])
        four_f = mix("four_f", [P, G, 2, 2 * P])
        conv_b = mix("conv_b", [P, 2, TOK])
        conv_c = mix("conv_c", [P, 2, TOK])
        conv_h = mix("conv_h", [P, 2, TOK])
        conv_z = mix("conv_z", [P, 2, G, P + 2])
        conv_wt = mix("conv_wt", [P, 2, 3])
        b_gate_sb = mix("b_gate_sb", [P, BANK])
        lev_e = mix("lev_e", [P, 2, HEADS, P])
        lev_q = mix("lev_q", [P, 2, HEADS, P])
        lev_k = mix("lev_k", [P, 2, HEADS, P])
        scores = mix("scores", [P, G, HEADS, P])
        o_sb = mix("o_sb", [P, HEADS, DK])
        o_ss = mix("o_ss", [P, HEADS])
        o_r = mix("o_r", [P, HEADS])
        scan_end = mix("scan_end", [P, HEADS, G])
        state_in = mix("state_in", [P, 2, HEADS, DK])
        h_tok = gates[:, 0, 0:2, :]
        pos_sb = gates[:, 0, 2, :]
        mask_in = gates[:, 1, :, :].rearrange("p b d -> p (b d)")[:, 0:N_MASK * P]
        merged = decay[:, :, :, :].rearrange("p a h t -> p (a h t)").rearrange("p (g d) -> p g d", g=G)
        a_t = q_t
        f_t = conv_c
        c_t = conv_h
        state_out = kgate[:, 0, :, :].rearrange("p h t -> p (h t)").rearrange("p (d h v) -> p d h v", d=2, h=HEADS)
        kd_sb = lev_k
        kd_t = lev_e
        scale2 = gates[:, 0, 0:2, :]
        h2_tok = gates[:, 1, 0:2, :]
        ln1_rows = [gates[:, 0, 2, :], gates[:, 1, 2, :]]
        hid_sh = mod_a[:, 0, 0:2 * TOK].rearrange("p (f t) -> p f t", f=2)
        silu_sh = mod_a[:, 1, 0:TOK]
        wide_tmp = tmp[:, :, :].rearrange("p h t -> p (h t)")
        mod_dram = nc.dram_tensor("mod_dram", [G, 6 * D], F32).ap()
        mixer_left = nc.sbuf_bytes_remaining
        mixer_sbuf.close()

        raw = ring[:, :, :].rearrange("p r n -> p (r n)").rearrange("p (s n) -> p s n", s=RAW)
        PIECE = 2 * D
        N_SPLIT = 4
        w_hi = moe("w_hi", [P, N_SPLIT, PIECE], F32R)
        w_lo = moe("w_lo", [P, N_SPLIT, PIECE], F32R)
        h_hi = moe("h_hi", [P, G, KD, P], F32R)
        h_lo = moe("h_lo", [P, G, KD, P], F32R)
        x_g = moe("x_g", [P, KD, ITEMS_PER_TURN, 2 * SLOTS], F32R)
        pick = moe("pick", [P, G, ITEMS_PER_TURN, 2 * SLOTS], F32R)
        gate4 = moe("gate4", [P, G, ITEMS_PER_TURN])
        slot_gate = moe("slot_gate", [SLOTS, ITEMS_PER_TURN])
        put_back = moe("put_back", [P, ITEMS_PER_TURN, G, P], F32R)
        gu_lo = moe("gu_lo", [SLOTS, 2 * DE])
        gu = moe("gu", [SLOTS, 2 * DE])
        silu_g = moe("silu_g", [SLOTS, DE])
        hid = moe("hid", [SLOTS, DE])
        hid_t = moe("hid_t", [P, 2, 2 * SLOTS], F32R)
        y_hi = moe("y_hi", [P, 2, BANK], F32R)
        y_lo = moe("y_lo", [P, 2, BANK], F32R)
        w_rt = moe("w_rt", [P, KD, N_EXP])
        b_rt = moe("b_rt", [P, N_EXP])
        score = moe("score", [P, G, N_EXP])
        biased = moe("biased", [P, G, N_EXP])
        left_over = moe("left_over", [P, G, N_EXP])
        top8 = moe("top8", [P, G, TOP_K])
        chosen = moe("chosen", [P, G, N_EXP])
        weight = moe("weight", [P, G, N_EXP])
        total_w = moe("total_w", [P, G])
        place = moe("place", [P, G, N_EXP])
        rows_t = moe("rows_t", [N_EXP, 2, G, P])
        first_item = moe("first_item", [N_EXP, MAX_CHUNKS])
        is_item = moe("is_item", [N_EXP, MAX_ITEMS])
        of_item = moe("of_item", [N_EXP, MAX_ITEMS])
        at_item = moe("at_item", [N_EXP, MAX_ITEMS])
        item_at = moe("item_at", [P, MAX_ITEMS])
        item_place = moe("item_place", [P, G, MAX_ITEMS])
        item_weight = moe("item_weight", [P, G, MAX_ITEMS])
        ln2_rows = [moe("ln2_g_row", [P, D]), moe("ln2_b_row", [P, D])]
        ctx.callback(experts_sbuf.close)

        bank = [ctx.enter_context(nc.psum_tensor(f"bank{n}", [P, BANK], F32)) for n in range(8)]
        product_bank, scratch_bank, o_bank = bank[0:3], bank[3:5], bank[5:7]
        acc_bank = [bank[5], bank[6], bank[7], bank[0]]
        gu_bank, turn_bank, y_bank = bank[1], bank[2], bank[3:5]
        gather_bank = [bank[1], bank[2], bank[3], bank[4]]

        ring_in = [sem(f"ring_in{n}") for n in range(RING)]
        chunk_used = sem("chunk_used")
        cond_in, cst_in, x_in, small_in = sem("cond_in"), sem("cst_in"), sem("x_in"), sem("small_in")
        b_ada_in = [sem("b_ada_in0"), sem("b_ada_in1")]
        mod_stored = [sem("mod_stored0"), sem("mod_stored1")]
        mod_in = [sem(f"mod_in{n}") for n in range(6)]
        b_gate_in = sem("b_gate_in")
        cond_ready = sem("cond_ready")
        product_ready = sem("product_ready")
        bank_free = [sem(f"bank_free{n}") for n in range(N_ROT)]
        scratch_ready = sem("scratch_ready")
        scratch_free = [sem("scratch_free0"), sem("scratch_free1")]
        var_ready, std_ready = sem("var_ready"), sem("std_ready")
        norm_ready = sem("norm_ready")
        lb_diff_ready, lb_exp_ready = sem("lb_diff_ready"), sem("lb_exp_ready")
        forget_split, forget_log = sem("forget_split"), sem("forget_log")
        diff_ready, exp_ready = sem("diff_ready"), sem("exp_ready")
        q_ready, k_ready, key_sum_ready = sem("q_ready"), sem("k_ready"), sem("key_sum_ready")
        start_exp_ready, start_q_ready = sem("start_exp_ready"), sem("start_q_ready")
        end_diff_ready, end_exp_ready, end_key_ready = sem("end_diff_ready"), sem("end_exp_ready"), sem("end_key_ready")
        conv_ready = sem("conv_ready")
        gate_sum_ready, gate_ready = sem("gate_sum_ready"), sem("gate_ready")
        o_ready, square_ready, ms_ready, rms_ready = sem("o_ready"), sem("square_ready"), sem("ms_ready"), sem("rms_ready")
        a_ready = sem("a_ready")
        merged_ready = sem("merged_ready")
        ln1_in = sem("ln1_in")
        state_stored = sem("state_stored")
        silu_sh_ready = sem("silu_sh_ready")
        dve_step, act_step = sem("dve_step"), sem("act_step")

        def evacuated(product):
            n = PRODUCT_NO[product]
            return bank_free[n % N_ROT], n // N_ROT + 1

        def read_out(use):
            n = SCRATCH_NO[use]
            return scratch_free[n % 2], n // 2 + 1

        def rotating(product):
            return product_bank[PRODUCT_NO[product] % N_ROT]

        def scratch(use):
            return scratch_bank[SCRATCH_NO[use] % 2]

        mixer_done = sem("mixer_done")
        router_in, ln2_in = sem("router_in"), sem("ln2_in")
        h_lo_ready = sem("h_lo_ready")
        split_ready = sem("split_ready")
        chosen_ready, counted, listed = sem("chosen_ready"), sem("counted"), sem("listed")
        score_ready = sem("score_ready")
        table_ready = sem("table_ready")
        piece_in = [sem(f"piece_in{n}") for n in range(RAW)]
        hi_ready, piece_used = sem("hi_ready"), sem("piece_used")
        low_up_ready, low_down_ready = sem("low_up_ready"), sem("low_down_ready")
        pick_ready, gathered = sem("pick_ready"), sem("gathered")
        x_even_ready, x_odd_ready = sem("x_even_ready"), sem("x_odd_ready")
        slot_gate_ready = sem("slot_gate_ready")
        gu_lo_ready, gu_sum_ready = sem("gu_lo_ready"), sem("gu_sum_ready")
        silu_ready, hid_ready = sem("silu_ready"), sem("hid_ready")
        turned, hid_hi_ready, hid_lo_ready, put_back_ready = sem("turned"), sem("hid_hi_ready"), sem("hid_lo_ready"), sem("put_back_ready")
        y0_ready, y_hi_ready, y_lo_ready, scattered = sem("y0_ready"), sem("y_hi_ready"), sem("y_lo_ready"), sem("scattered")
        split_free = sem("split_free")
        moe_done, out_ready, out_stored = sem("moe_done"), sem("out_ready"), sem("out_stored")

        def tok(g):
            return slice(g * P, (g + 1) * P)

        def rows8(w):
            return w.rearrange("(p k) n -> p k n", k=KD)

        def tiles(w):
            return w.rearrange("(k p) n -> p k n", p=P)

        def row(v):
            return v.partition_broadcast(P)

        def turns_after_first(eng):
            eng.wait_ge(table_ready, 2)
            return eng.value_load(last_turn[0:1, 0:1], min_val=1, max_val=MAX_ITEMS // ITEMS_PER_TURN - 1)

        block = ctx.enter_context(nc.Block())

        @block.sync
        def _(sp):
            def weights(n, chunk):
                kind, c = chunk
                slot = ring[:, n % RING, :]
                by_k = slot.rearrange("p (k n) -> p k n", k=KD)
                s = ring_in[n % RING]
                cols = slice(c * BANK, (c + 1) * BANK)
                if kind == "ada":
                    sp.dma_start(by_k, rows8(w_ada[0])[:, :, cols]).then_inc(s, 16)
                elif kind == "in":
                    sp.dma_start(by_k, tiles(w_in[0])[:, :, cols]).then_inc(s, 16)
                elif kind == "proj_hgrn":
                    sp.dma_start(slot.rearrange("p (k n) -> p k n", k=HEADS), tiles(w_proj_hgrn[0])).then_inc(s, 16)
                elif kind == "proj_fc":
                    half = slot.rearrange("p (b k n) -> p b k n", b=2, k=2)
                    sp.dma_start(half[:, 0], tiles(w_proj_fourier[0])).then_inc(s, 16)
                    sp.dma_start(half[:, 1], tiles(w_proj_conv[0])).then_inc(s, 16)
                elif kind == "out":
                    sp.dma_start(by_k, tiles(w_out[0])[:, :, cols]).then_inc(s, 16)
                elif kind == "shared_up":
                    half = slot.rearrange("p (b k n) -> p b k n", b=2, k=KD)
                    sp.dma_start(half[:, 0], rows8(w_sh_gate[0])).then_inc(s, 16)
                    sp.dma_start(half[:, 1], rows8(w_sh_up[0])).then_inc(s, 16)
                else:
                    sp.dma_start(slot[:, 0:2 * D].rearrange("p (k n) -> p k n", k=2), tiles(w_sh_down[0])).then_inc(s, 16)

            for n, chunk in enumerate(CHUNKS):
                if n >= RING:
                    sp.wait_ge(chunk_used, n - RING + 1)
                weights(n, chunk)

            def piece(kind, p, e):
                s = raw_slot(p)
                at = raw[:, s, :]
                if kind == "down":
                    src = w_exp_down[0, bass.ds(e, 1)].rearrange("a (p f) n -> p (a f) n", f=2)
                    for f in range(2):
                        sp.dma_start(at[:, f * D:(f + 1) * D], src[:, f]).then_inc(piece_in[s], 16)
                else:
                    ks = slice(kind * KD // 2, (kind + 1) * KD // 2)
                    for b, w in enumerate((w_exp_gate, w_exp_up)):
                        src = w[0, bass.ds(e, 1)].rearrange("a (p k) n -> p (a k) n", k=KD)
                        sp.dma_start(at[:, b * D:(b + 1) * D].rearrange("p (k n) -> p k n", n=DE),
                                     src[:, ks]).then_inc(piece_in[s], 16)

            def expert_of(n):
                return sp.value_load(item_expert[0:1, bass.ds(val(n), 1)], min_val=0, max_val=N_EXP - 1)

            def free(kind, n, p):
                if above_zero(p - RAW + 1):
                    if kind == "down":
                        sp.wait_ge(low_down_ready, val(n - 2))
                    else:
                        sp.wait_ge(low_up_ready, val(2 * (n - 2) + kind + 1))
                else:
                    sp.wait_ge(chunk_used, len(CHUNKS) - RING + 1 + p // 2)

            more_turns = turns_after_first(sp)

            def turn(j, first):
                e_before = None if first else expert_of(j * ITEMS_PER_TURN - 1)
                for q in range(ITEMS_PER_TURN):
                    e = expert_of(j * ITEMS_PER_TURN + q)
                    for kind, c in ((0, -1), (1, 0)):
                        c = 3 * q + c + (first and q == 0)
                        free(kind, j * ITEMS_PER_TURN + q, 12 * j + c)
                        piece(kind, (j, c), e)
                    if not (first and q == 0):
                        c = 3 * q + 1
                        free("down", j * ITEMS_PER_TURN + q, 12 * j + c)
                        piece("down", (j, c), e_before)
                    e_before = e
            turn(0, True)
            with sp.Fori(0, more_turns) as t:
                turn(Count(t, 1, 1), False)
            turns = Count(more_turns, 1, 1)
            e = expert_of(turns * ITEMS_PER_TURN - 1)
            free("down", turns * ITEMS_PER_TURN, 12 * turns - 1)
            piece("down", (turns, -1), e)

            for g, y in enumerate((y_prompt, y_sample)):
                sp.wait_ge(out_ready, g + 1)
                sp.dma_start(y[0], resid[:, g, :]).then_inc(out_stored, 16)
            sp.wait_ge(state_stored, 32)
            sp.wait_ge(out_stored, 32)

        @block.gpsimd
        def _(pool):
            def store_row(n):
                c = (ADA_EARLY + ADA_LATE)[n]
                if n + 1 < 2 * len(ADA_EARLY):
                    nxt = (ADA_EARLY + ADA_LATE)[n + 1]
                    if n >= 1:
                        pool.wait_ge(*evacuated(("ada", (ADA_EARLY + ADA_LATE)[n - 1])))
                    load_bias(n + 1, nxt)
                pool.wait_ge(*evacuated(("ada", c)))
                nc.gpsimd.dma_start(mod_dram[:, c * BANK:(c + 1) * BANK], mod_row[:, n % 2, :]).then_inc(mod_stored[n % 2], 16)

            def load_bias(n, c):
                nc.gpsimd.dma_start(b_ada_sb[:, n % 2, :], b_ada[:, c * BANK:(c + 1) * BANK].rearrange("a n -> (a n)").partition_broadcast(G)).then_inc(b_ada_in[n % 2], 16)

            def spread(v, dst):
                for s in mod_stored:
                    pool.wait_ge(s, 16 * (v + 1))
                for g in range(G):
                    nc.gpsimd.dma_start(dst[:, g, :], row(mod_dram[g, v * D:(v + 1) * D])).then_inc(mod_in[v], 16)

            load_bias(0, 0)
            for n in range(len(ADA_EARLY)):
                store_row(n)
                if n == 1:
                    spread(0, mod_a)
                if n == 3:
                    spread(1, mod_b)
            pool.wait_ge(norm_ready, G)
            spread(2, mod_a)

            late = len(ADA_EARLY)
            for what, at in schedule():
                if what == "step":
                    d, g, n = STEPS[at]
                    if d is not None:
                        pool.wait_ge(exp_ready, at + 1)
                        if at >= 2:
                            pool.wait_ge(scratch_ready, SCRATCH_NO[("step", at - 2)] + 1)
                        nc.gpsimd.tensor_tensor(lev_k[:, at % 2], kgate[:, d, :, tok(g)], lev_e[:, at % 2],
                                                ALU.mult).then_inc(k_ready, 1)
                elif at[0] == "ada":
                    store_row(late)
                    if late == 7:
                        spread(3, mod_b)
                    late += 1
                elif at[1] >= 7 and at[2] == 0:
                    if at[1] > 7:
                        pool.wait_ge(*evacuated(("in", at[1] - 1, 1)))
                    c = at[1] - 7
                    nc.gpsimd.dma_start(b_gate_sb[:, :], row(b_gate[0, c * BANK:(c + 1) * BANK])).then_inc(b_gate_in, 16)
            spread(5, gate2)
            pool.wait_ge(merged_ready, 2 * G)
            spread(4, scale2)
            nc.gpsimd.drain().then_inc(mixer_done, 1)

            def low_down(j, c):
                p = 12 * j + c
                s = raw_slot((j, c))
                pool.wait_ge(piece_in[s], val(32 * (2 * j + c // RAW + 1)))
                pool.wait_ge(hi_ready, val(p + 1))
                if above_zero(p - N_SPLIT + 1):
                    pool.wait_ge(piece_used, val(p - N_SPLIT + 1))
                nc.gpsimd.tensor_tensor(w_lo[:, c % N_SPLIT, :], raw[:, s, :], w_hi[:, c % N_SPLIT, :].bitcast(F32),
                                        ALU.subtract).then_inc(low_down_ready, 1)

            def turn(j, first):
                for q in range(first, ITEMS_PER_TURN):
                    low_down(j, 3 * q + 1)

            pool.wait_ge(split_free, 1)
            more_turns = turns_after_first(pool)
            turn(0, True)
            with pool.Fori(0, more_turns) as t:
                turn(Count(t, 1, 1), False)
            low_down(Count(more_turns, 1, 1), -1)

        @block.scalar
        def _(act):
            own = [0]

            def step(ins):
                ins.then_inc(act_step, 1)
                own[0] += 1
                act.wait_ge(act_step, own[0])

            act.dma_start(cond_t[:, 0, :], c_ctx.rearrange("(p k) -> p k", k=KD)).then_inc(cond_in, 16)
            act.dma_start(cond_t[:, 1, :], c[0].rearrange("(p k) -> p k", k=KD)).then_inc(cond_in, 16)
            act.dma_start(resid[:, 0, :], x_prompt[0]).then_inc(x_in, 16)
            act.dma_start(resid[:, 1, :], x_sample[0]).then_inc(x_in, 16)
            act.dma_start(pos_sb, pos).then_inc(x_in, 16)
            act.dma_start(cst[:, :], table[:, 0:CST_KEEP]).then_inc(cst_in, 16)
            act.dma_start(dft[:, :], table[:, CST_KEEP:]).then_inc(small_in, 16)
            act.dma_start(mask_in, masks).then_inc(small_in, 16)
            act.dma_start(lb_in[:, :].rearrange("p (d h) -> p d h", d=2), hgrn_lb[0].rearrange("d (h p) -> p d h", p=P), allow_slow_non_contiguous=True).then_inc(small_in, 16)
            act.dma_start(norm_row[:, :], row(hgrn_norm[0])).then_inc(small_in, 16)
            for ct in range(2):
                act.dma_start(conv_wt[:, ct, :], conv_w[0, :, ct * P:(ct + 1) * P].rearrange("k p -> p k"), allow_slow_non_contiguous=True).then_inc(small_in, 16)
            act.dma_start(state_in[:, :, :, :].rearrange("p d h v -> p (d h) v"),
                          state_hgrn[0, 0].rearrange("d h k v -> k (d h) v")).then_inc(small_in, 16)

            act.wait_ge(cond_in, 32)
            nc.scalar.activation(cond_s[:, :, :], cond_t[:, :, :].rearrange("p g k -> p k g"), ACT.Silu).then_inc(cond_ready, 1)

            def deviation(n):
                act.wait_ge(var_ready, n + 1)
                nc.scalar.activation(std[:, :], vareps[:, :], ACT.Sqrt).then_inc(std_ready, 1)

            def from_scratch(use, out, func=ACT.Copy):
                n = SCRATCH_NO[use]
                act.wait_ge(scratch_ready, n + 1)
                nc.scalar.activation(out, scratch(use)[:, 0:out.free_size()] if len(out.shape) == 2 else
                                     scratch(use)[:, 0:out.free_size()].rearrange("p (a b) -> p a b", a=out.shape[1]),
                                     func).then_inc(scratch_free[n % 2], 1)

            deviation(0)
            deviation(1)
            for g in range(G):
                for a in range(2):
                    from_scratch(("h", g, a), h_t[:, 4 * a:4 * a + 4, tok(g)])
            act.wait_ge(lb_diff_ready, 1)
            nc.scalar.activation(lb_e[:, :], lb_e[:, :], ACT.Exp).then_inc(lb_exp_ready, 1)

            def product_out(at):
                _, c, h = at
                n = PRODUCT_NO[at]
                act.wait_ge(product_ready, n + 1)
                b = rotating(at)
                pair = b[:, :].rearrange("p (a t) -> p a t", a=2)
                free = bank_free[n % N_ROT]
                if c in (2, 3):
                    nc.scalar.activation(fgate[:, c - 2, 2 * h:2 * h + 2, :], pair, ACT.Sigmoid)
                    nc.scalar.activation(kgate[:, c - 2, 2 * h:2 * h + 2, :], pair, ACT.Sigmoid, scale=-1.0).then_inc(free, 1)
                elif c == 0:
                    nc.scalar.activation(q_t[:, 2 * h:2 * h + 2, :], pair, ACT.Silu).then_inc(free, 1)
                elif c == 1:
                    nc.scalar.activation(value[:, h, :], b[:, :], ACT.Copy).then_inc(free, 1)
                elif c == 4:
                    nc.scalar.activation(out_gate[:, h, :], b[:, :], ACT.Silu).then_inc(free, 1)
                else:
                    out = {(5, 0): four, (5, 1): conv_b, (6, 0): conv_c, (6, 1): conv_h}[c, h]
                    nc.scalar.activation(out[:, :, :], pair, ACT.Copy).then_inc(free, 1)

            def forget_logs(d):
                act.wait_ge(forget_split, d + 1)
                both = decay[:, d, :, :].rearrange("p h t -> p (h t)")
                nc.scalar.activation(both, both, ACT.Ln)
                nc.scalar.activation(wide_tmp, wide_tmp, ACT.Ln, scale=1.0 / LN_SPLIT).then_inc(forget_log, 1)

            for what, at in schedule():
                if what == "step":
                    d, g, n = STEPS[at]
                    if d is not None:
                        act.wait_ge(diff_ready, at + 1)
                        nc.scalar.activation(lev_e[:, at % 2], lev_e[:, at % 2], ACT.Exp).then_inc(exp_ready, 1)
                elif at[0] == "in" and at[1] < 7:
                    product_out(at)
                    if at == ("in", 0, 1):
                        forget_logs(0)
                    if at == ("in", 1, 1):
                        forget_logs(1)

            n_scan = 2 * G * len(LEVELS)
            act.wait_ge(q_ready, n_scan)
            act.wait_ge(k_ready, n_scan)
            for d in range(2):
                nc.scalar.activation(lev_e[:, d], fgate[:, d, :, tok(1)], ACT.Exp).then_inc(start_exp_ready, 1)
            for d in range(2):
                act.wait_ge(end_diff_ready, d + 1)
                nc.scalar.activation(lev_e[:, d], lev_e[:, d], ACT.Exp).then_inc(end_exp_ready, 1)
            for g in range(G):
                from_scratch(("four1", g), four_f[:, g])
            for d in range(2):
                act.wait_ge(end_key_ready, 2)
                from_scratch(("ends", d), kd_t[:, d])
            for d in range(2):
                from_scratch(("state", d), state_out[:, d])
            for d in range(2):
                act.wait_ge(*read_out(("state", d)))
                act.dma_start(state_new[0, 0, d].rearrange("h k v -> k h v"), state_out[:, d]).then_inc(state_stored, 16)
            act.wait_ge(conv_ready, 1)
            from_scratch(("four2",), f_t[:, :, :])
            act.wait_ge(*evacuated(("in", 12, 1)))
            for g in range(G):
                g_all = gates[:, g].rearrange("p b d -> p (b d)")
                nc.scalar.activation(g_all, g_all, ACT.Sigmoid).then_inc(gate_ready, 1)
            for g in range(G):
                act.wait_ge(o_ready, g + 1)
                if g:
                    act.wait_ge(ms_ready, g)
                nc.scalar.activation(tmp[:, :, 0:P], o_bank[g][:, :].rearrange("p (h v) -> p h v", h=HEADS),
                                     ACT.Square).then_inc(square_ready, 1)
                act.wait_ge(ms_ready, g + 1)
                nc.scalar.activation(o_ss[:, :], o_ss[:, :], ACT.Sqrt).then_inc(rms_ready, 1)
            for g in range(G):
                from_scratch(("a", g), a_t[:, :, tok(g)])
            for g in range(G):
                for a in range(2):
                    from_scratch(("merged", g, a), h_t[:, 4 * a:4 * a + 4, tok(g)])
            act.wait_ge(merged_ready, 2 * G)
            act.dma_start(ln1_rows[0], row(ln1_g[0])).then_inc(ln1_in, 16)
            act.dma_start(ln1_rows[1], row(ln1_b[0])).then_inc(ln1_in, 16)
            act.wait_ge(state_stored, 32)
            act.drain().then_inc(mixer_done, 1)

            act.wait_ge(mixer_done, 4)
            act.dma_start(w_rt[:, :, :], rows8(w_router[0])).then_inc(router_in, 16)
            act.dma_start(b_rt[:, :], row(b_router[0])).then_inc(router_in, 16)
            act.dma_start(ln2_rows[0][:, :], row(ln2_g[0])).then_inc(ln2_in, 16)
            act.dma_start(ln2_rows[1][:, :], row(ln2_b[0])).then_inc(ln2_in, 16)
            for n in range(2, 6):
                deviation(n)
            act.wait_ge(norm_ready, 2 * G)
            for g in range(G):
                nc.scalar.activation(h_hi[:, g], h2_tok[:, g, :].rearrange("p (q k) -> p k q", k=KD),
                                     ACT.Copy).then_inc(split_ready, 1)
            for g in range(G):
                for a in range(2):
                    from_scratch(("h2", g, a), h_t[:, 4 * a:4 * a + 4, tok(g)])
            for f in range(2):
                act.wait_ge(product_ready, PRODUCT_NO[("shared", f)] + 1)
                if f:
                    act.wait_ge(*evacuated(("shared", f - 1)))
                nc.scalar.activation(silu_sh, rotating(("shared", f))[:, 0:TOK], ACT.Silu).then_inc(silu_sh_ready, 1)
            act.wait_ge(mixer_done, 4)
            from_scratch(("logits",), score[:, :, :], ACT.Sigmoid)
            act.wait_ge(scratch_ready, SCRATCH_NO[("rows",)] + 1)
            nc.scalar.activation(rows_t[:, :, :, :].rearrange("p a g t -> p (a g t)"),
                                 scratch(("rows",))[0:N_EXP, :], ACT.Copy).then_inc(scratch_free[SCRATCH_NO[("rows",)] % 2], 1)

            def high(j, c, kind):
                p = 12 * j + c
                s = raw_slot((j, c))
                act.wait_ge(piece_in[s], val(32 * (2 * j + c // RAW + 1)))
                if above_zero(p - N_SPLIT + 1):
                    act.wait_ge(piece_used, val(p - N_SPLIT + 1))
                out, src = w_hi[:, c % N_SPLIT, :], raw[:, s, :]
                if kind == "up":
                    out = out.rearrange("p (k b n) -> p k b n", k=KD // 2, b=2)
                    src = src.rearrange("p (b k n) -> p k b n", k=KD // 2, b=2)
                nc.scalar.activation(out, src, ACT.Copy).then_inc(hi_ready, 1)

            def need(s, value):
                if above_zero(value):
                    act.wait_ge(s, val(value))

            def turned_out(n, q, first):
                act.wait_ge(turned, val(n + 1))
                if q is not None:
                    need(scattered, n - 3)
                    nc.scalar.activation(put_back[:, q], turn_bank[:, P:P + G * P].rearrange("p (g t) -> p g t", g=G),
                                         ACT.Copy).then_inc(put_back_ready, 1)
                if not first:
                    nc.scalar.activation(hid_t[:, :, 0:SLOTS], turn_bank[:, 0:2 * SLOTS].rearrange("p (f s) -> p f s", f=2),
                                         ACT.Copy).then_inc(hid_hi_ready, 1)

            def y_high(m, h, last=False):
                if h == 0:
                    act.wait_ge(y0_ready, val(m + 1))
                else:
                    act.wait_ge(piece_used, val(3 * m + (3 if last else 5)))
                need(scattered, m)
                nc.scalar.activation(y_hi[:, h, :], y_bank[h][:, :], ACT.Copy).then_inc(y_hi_ready, 1)

            def gu_low(m):
                act.wait_ge(piece_used, val(3 * m + 1 if above_zero(m) else 2))
                need(gu_sum_ready, m)
                nc.scalar.activation(gu_lo[:, :], gu_bank[SLOTS:2 * SLOTS, :], ACT.Copy).then_inc(gu_lo_ready, 1)

            def silu(m):
                act.wait_ge(gu_sum_ready, val(m + 1))
                nc.scalar.activation(silu_g[:, :], gu[:, 0:DE], ACT.Silu).then_inc(silu_ready, 1)

            def gather_out(j):
                act.wait_ge(gathered, val((KD + 1) * j + 1))
                need(hid_ready, j * ITEMS_PER_TURN)
                nc.scalar.activation(slot_gate[:, :], gather_bank[0][0:SLOTS, 0:ITEMS_PER_TURN], ACT.Copy).then_inc(slot_gate_ready, 1)
                for k in range(0, KD, 2):
                    act.wait_ge(gathered, val((KD + 1) * j + k + 2))
                    nc.scalar.activation(x_g[:, k], gather_bank[(k + 1) % 4][:, :].rearrange("p (q s) -> p q s", q=ITEMS_PER_TURN),
                                         ACT.Copy).then_inc(x_even_ready, 1)

            def turn(j, first):
                for q in range(ITEMS_PER_TURN):
                    n = j * ITEMS_PER_TURN + q
                    start = first and q == 0
                    high(j, 3 * q - 1 + start, "up")
                    high(j, 3 * q + start, "up")
                    if not start:
                        gu_low(n - 1)
                        turned_out(n - 1, (q - 1) % ITEMS_PER_TURN, first and q == 1)
                        silu(n - 1)
                        high(j, 3 * q + 1, "down")
                        if not (first and q == 1):
                            for h in range(2):
                                y_high(n - 2, h)
                    if q == 0:
                        gather_out(j)

            act.wait_ge(split_free, 1)
            more_turns = turns_after_first(act)
            turn(0, True)
            with act.Fori(0, more_turns) as t:
                turn(Count(t, 1, 1), False)
            turns = Count(more_turns, 1, 1)
            n_items = turns * ITEMS_PER_TURN
            gu_low(n_items - 1)
            turned_out(n_items - 1, ITEMS_PER_TURN - 1, False)
            silu(n_items - 1)
            high(turns, -1, "down")
            for h in range(2):
                y_high(n_items - 2, h)
            turned_out(n_items, None, False)
            for h in range(2):
                y_high(n_items - 1, h, True)
            for n in range(6, 8):
                deviation(n)

        @block.vector
        def _(dve):
            own = [0]

            def step(ins):
                ins.then_inc(dve_step, 1)
                own[0] += 1
                dve.wait_ge(dve_step, own[0])

            def need(s, value):
                if above_zero(value):
                    dve.wait_ge(s, val(value))

            norms = [0]

            def normalize(out, x):
                n = norms[0]
                norms[0] += 1
                for h in range(2):
                    ins = nc.vector.bn_stats(bn[:, h, :], x[:, h * BANK:(h + 1) * BANK])
                step(ins)
                step(nc.vector.bn_aggr(mv[:, :], bn[:, :, :]))
                nc.vector.tensor_scalar(vareps[:, :], mv[:, 1:2], LN_EPS, None, ALU.add).then_inc(var_ready, 1)
                dve.wait_ge(std_ready, n + 1)
                step(nc.vector.reciprocal(rstd[:, :], std[:, :]))
                step(nc.vector.tensor_scalar(out, x, mv[:, 0:1], rstd[:, 0:1], ALU.subtract, ALU.mult))

            dve.wait_ge(x_in, 48)
            step(nc.vector.tensor_tensor(resid[:, 1, :], resid[:, 1, :], pos_sb, ALU.add))
            for g in range(G):
                normalize(h_tok[:, g, :], resid[:, g, :])
            for e in (0, P + 1):
                nc.vector.memset(conv_z[:, :, :, e:e + 1], 0.0)

            def modulation_row(n, c):
                dve.wait_ge(product_ready, PRODUCT_NO[("ada", c)] + 1)
                dve.wait_ge(b_ada_in[n % 2], 16 * (n // 2 + 1))
                if n >= 2:
                    dve.wait_ge(mod_stored[n % 2], 16 * (n // 2))
                nc.vector.tensor_tensor(mod_row[:, n % 2, :], rotating(("ada", c))[0:G, :], b_ada_sb[:, n % 2, :],
                                        ALU.add).then_inc(evacuated(("ada", c))[0], 1)

            for n in range(4):
                modulation_row(n, ADA_EARLY[n])
            dve.wait_ge(mod_in[0], 32)
            dve.wait_ge(mod_in[1], 32)
            for g in range(G):
                step(nc.vector.scalar_tensor_tensor(h_tok[:, g, :], mod_b[:, g, :], 1.0, h_tok[:, g, :], ALU.add, ALU.mult))
                nc.vector.tensor_tensor(h_tok[:, g, :], h_tok[:, g, :], mod_a[:, g, :], ALU.add).then_inc(norm_ready, 1)
            for n in range(4, 6):
                modulation_row(n, ADA_EARLY[n])

            dve.wait_ge(small_in, 7 * 16)
            nc.vector.tensor_copy(mask_sb[:, :, :].rearrange("p m t -> p (m t)"), mask_in)
            nc.vector.tensor_tensor(lb_e[:, :], lb_in[:, :], lb_in[:, :], ALU.subtract).then_inc(lb_diff_ready, 1)
            dve.wait_ge(lb_exp_ready, 1)
            step(nc.vector.reciprocal(lb[:, :], lb_e[:, :]))
            step(nc.vector.tensor_tensor(lb_one[:, :], lb_e[:, :], lb[:, :], ALU.mult))
            step(nc.vector.tensor_tensor(lb[:, :], lb_one[:, :], lb_one[:, :], ALU.subtract))
            step(nc.vector.tensor_scalar(lb_one[:, :], lb[:, :], -1.0, 1.0, ALU.mult, ALU.add))

            def forget(d):
                for h in range(2):
                    dve.wait_ge(*evacuated(("in", 2 + d, h)))
                for h in range(HEADS):
                    b = d * HEADS + h
                    nc.vector.tensor_scalar(fgate[:, d, h, :], fgate[:, d, h, :], lb_one[:, b:b + 1], lb[:, b:b + 1], ALU.mult, ALU.add)
                    ins = nc.vector.tensor_scalar(kgate[:, d, h, :], kgate[:, d, h, :], lb_one[:, b:b + 1], None, ALU.mult)
                step(ins)
                f_all = fgate[:, d, :, :].rearrange("p h t -> p (h t)")
                log_all = decay[:, d, :, :].rearrange("p h t -> p (h t)")
                nc.vector.tensor_scalar(log_all, f_all, LN_SPLIT, None, ALU.max)
                nc.vector.tensor_scalar(wide_tmp, f_all, F_MIN, LN_SPLIT, ALU.max, ALU.min).then_inc(forget_split, 1)
                dve.wait_ge(forget_log, d + 1)
                step(nc.vector.tensor_tensor(log_all, log_all, wide_tmp, ALU.add))
                for h in range(HEADS):
                    for g in range(G):
                        ins = nc.vector.tensor_tensor_scan(fgate[:, d, h, tok(g)], ones, decay[:, d, h, tok(g)], 0.0, ALU.mult, ALU.add)
                step(ins)
                if d == 1:
                    step(nc.vector.tensor_copy(scan_end[:, :, :], fgate[:, 1].rearrange("p h (g t) -> p h g t", g=G)[:, :, :, P - 1]))
                    step(nc.vector.tensor_tensor(f_all, log_all, f_all, ALU.subtract))
                    for h in range(HEADS):
                        for g in range(G):
                            ins = nc.vector.tensor_scalar(fgate[:, 1, h, tok(g)], fgate[:, 1, h, tok(g)], scan_end[:, h, g:g + 1], None, ALU.add)
                    step(ins)

            forget(0)
            forget(1)

            def level_diffs(s):
                d, g, n = STEPS[s]
                half = LEVELS[n]
                b = fgate[:, d, :, tok(g)].rearrange("p h (m a i) -> p h m a i", a=2, i=half)
                e = lev_e[:, s % 2].rearrange("p h (m a i) -> p h m a i", a=2, i=half)
                at = b[:, :, :, 0, half - 1:half] if d == 0 else b[:, :, :, 1, 0:1]
                mid = at.broadcast_to([P, HEADS, P // (2 * half), half])
                below, above = (0, 1) if d == 0 else (1, 0)
                if s >= 2:
                    dve.wait_ge(k_ready, s - 1)
                nc.vector.tensor_tensor(e[:, :, :, below, :], mid, b[:, :, :, below, :], ALU.subtract)
                nc.vector.tensor_tensor(e[:, :, :, above, :], b[:, :, :, above, :], mid, ALU.subtract).then_inc(diff_ready, 1)

            def take_scores(s):
                d, g, n = STEPS[s]
                m = N_MASK - 1 if d is None else d * len(LEVELS) + n
                use = SCRATCH_NO[("step", s)]
                dve.wait_ge(scratch_ready, use + 1)
                nc.vector.copy_predicated(scores[:, g], mask_sb[:, m:m + 1, :].broadcast_to([P, HEADS, P]),
                                          scratch(("step", s))[:, :].rearrange("p (h t) -> p h t", h=HEADS)).then_inc(scratch_free[use % 2], 1)

            def scan_step(s):
                d, g, n = STEPS[s]
                if d is not None:
                    level_diffs(s)
                if s:
                    take_scores(s - 1)
                if d is None:
                    nc.vector.tensor_tensor(lev_k[:, s % 2], kgate[:, 0, :, tok(g)], kgate[:, 1, :, tok(g)], ALU.add).then_inc(key_sum_ready, 1)
                else:
                    dve.wait_ge(exp_ready, s + 1)
                    nc.vector.tensor_tensor(lev_q[:, s % 2], q_t[:, :, tok(g)], lev_e[:, s % 2], ALU.mult).then_inc(q_ready, 1)

            def convolution():
                for p in [("in", 5, 1), ("in", 6, 0), ("in", 6, 1)]:
                    dve.wait_ge(*evacuated(p))
                by_g = lambda t, ct: t[:, ct, :].rearrange("p (g t) -> p g t", g=G)
                for ct in range(2):
                    ins = nc.vector.tensor_tensor(conv_z[:, ct, :, 1:P + 1], by_g(conv_c, ct), by_g(conv_h, ct), ALU.mult)
                step(ins)
                for tap in (1, 0, 2):
                    for ct in range(2):
                        z, y, w = conv_z[:, ct, :, tap:tap + P], by_g(c_t, ct), conv_wt[:, ct, tap:tap + 1]
                        if tap == 1:
                            ins = nc.vector.tensor_scalar(y, z, w, None, ALU.mult)
                        else:
                            ins = nc.vector.scalar_tensor_tensor(y, z, w, y, ALU.mult, ALU.add)
                    step(ins)
                nc.vector.tensor_tensor(c_t[:, :, :], c_t[:, :, :], conv_b[:, :, :], ALU.mult).then_inc(conv_ready, 1)

            late = 6
            for what, at in schedule():
                if what == "step":
                    if at == 0:
                        for h in range(2):
                            dve.wait_ge(*evacuated(("in", 0, h)))
                    scan_step(at)
                elif at[0] == "ada":
                    modulation_row(late, at[1])
                    late += 1
                elif at[1] >= 7:
                    if at == ("in", 7, 0):
                        convolution()
                    _, c, g = at
                    b, h = (c - 7) // 2, (c - 7) % 2
                    dve.wait_ge(product_ready, PRODUCT_NO[at] + 1)
                    dve.wait_ge(b_gate_in, 16 * (c - 6))
                    nc.vector.tensor_tensor(gates[:, g, b, h * BANK:(h + 1) * BANK], rotating(at)[:, :], b_gate_sb[:, :],
                                            ALU.add).then_inc(evacuated(at)[0], 1)
            take_scores(len(STEPS) - 1)

            for d in range(2):
                dve.wait_ge(start_exp_ready, d + 1)
                nc.vector.tensor_tensor(lev_q[:, d], q_t[:, :, tok(1)], lev_e[:, d], ALU.mult).then_inc(start_q_ready, 1)
            dve.wait_ge(start_q_ready, 2)
            for d in range(2):
                end = P - 1 if d == 0 else 0
                b = fgate[:, d, :, tok(0)]
                nc.vector.tensor_tensor(lev_e[:, d], b[:, :, end:end + 1].broadcast_to([P, HEADS, P]), b, ALU.subtract).then_inc(end_diff_ready, 1)
            for d in range(2):
                dve.wait_ge(end_exp_ready, d + 1)
                nc.vector.tensor_tensor(kd_sb[:, d], kgate[:, d, :, tok(0)], lev_e[:, d], ALU.mult).then_inc(end_key_ready, 1)

            for g in range(G):
                step(nc.vector.tensor_tensor(out_gate[:, g, :], out_gate[:, g, :], norm_row[:, :], ALU.mult))
            for g in range(G):
                dve.wait_ge(square_ready, g + 1)
                step(nc.vector.reduce_sum(o_ss[:, :], tmp[:, :, 0:P], axis=AXX))
                nc.vector.tensor_scalar(o_ss[:, :], o_ss[:, :], 1.0 / DK, RMS_EPS, ALU.mult, ALU.add).then_inc(ms_ready, 1)
                dve.wait_ge(rms_ready, g + 1)
                step(nc.vector.reciprocal(o_r[:, :], o_ss[:, :]))
                if g:
                    dve.wait_ge(scratch_ready, SCRATCH_NO[("a", g - 1)] + 1)
                step(nc.vector.tensor_tensor(o_sb[:, :, :], o_bank[g][:, :].rearrange("p (h v) -> p h v", h=HEADS),
                                             o_r[:, :].unsqueeze(2).broadcast_to([P, HEADS, DK]), ALU.mult))
                nc.vector.tensor_tensor(o_sb[:, :, :], o_sb[:, :, :], out_gate[:, g, :].rearrange("p (h v) -> p h v", h=HEADS),
                                        ALU.mult).then_inc(a_ready, 1)

            for g in range(G):
                dve.wait_ge(gate_ready, g + 1)
                for h in range(2):
                    cols = slice(h * BANK, (h + 1) * BANK)
                    for b in range(NB):
                        at = ("proj", g, h, b)
                        s, full = evacuated(at)
                        dve.wait_ge(product_ready, PRODUCT_NO[at] + 1)
                        out = merged[:, g, cols] if b == 0 else wide_tmp[:, 0:BANK]
                        nc.vector.tensor_tensor(out, rotating(at)[:, :], gates[:, g, b, cols], ALU.mult).then_inc(s, 1)
                        dve.wait_ge(s, full)
                        if b:
                            ins = nc.vector.tensor_tensor(merged[:, g, cols], merged[:, g, cols], wide_tmp[:, 0:BANK], ALU.add)
                            if b < NB - 1:
                                step(ins)
                    ins.then_inc(merged_ready, 1)
                    dve.wait_ge(merged_ready, 2 * g + h + 1)

            dve.wait_ge(mod_in[2], 32)
            for h in range(2):
                cols = slice(h * BANK, (h + 1) * BANK)
                for g in range(G):
                    at = ("out", h, g)
                    s, full = evacuated(at)
                    dve.wait_ge(product_ready, PRODUCT_NO[at] + 1)
                    nc.vector.tensor_tensor(mod_a[:, g, cols], rotating(at)[:, :], mod_a[:, g, cols], ALU.mult).then_inc(s, 1)
                    dve.wait_ge(s, full)
                    step(nc.vector.scalar_tensor_tensor(resid[:, g, cols], resid[:, g, cols], ALPHA, mod_a[:, g, cols], ALU.mult, ALU.add))
            nc.vector.drain().then_inc(mixer_done, 1)
            dve.wait_ge(ln1_in, 32)
            for g in range(G):
                normalize(resid[:, g, :], resid[:, g, :])
                step(nc.vector.tensor_tensor(resid[:, g, :], resid[:, g, :], ln1_rows[0], ALU.mult))
                step(nc.vector.tensor_tensor(resid[:, g, :], resid[:, g, :], ln1_rows[1], ALU.add))
            dve.wait_ge(mod_in[3], 32)
            dve.wait_ge(mod_in[4], 32)
            for g in range(G):
                normalize(h2_tok[:, g, :], resid[:, g, :])
                step(nc.vector.scalar_tensor_tensor(h2_tok[:, g, :], scale2[:, g, :], 1.0, h2_tok[:, g, :], ALU.add, ALU.mult))
                nc.vector.tensor_tensor(h2_tok[:, g, :], h2_tok[:, g, :], mod_b[:, g, :], ALU.add).then_inc(norm_ready, 1)
            dve.wait_ge(norm_ready, 2 * G)
            dve.wait_ge(mixer_done, 4)
            for g in range(G):
                dve.wait_ge(split_ready, g + 1)
                nc.vector.tensor_tensor(h_lo[:, g], h2_tok[:, g, :].rearrange("p (q k) -> p k q", k=KD), h_hi[:, g].bitcast(F32), ALU.subtract).then_inc(h_lo_ready, 1)
            for f in range(2):
                at = ("shared", f)
                dve.wait_ge(silu_sh_ready, f + 1)
                nc.vector.tensor_tensor(hid_sh[:, f, :], silu_sh, rotating(at)[:, TOK:2 * TOK], ALU.mult).then_inc(evacuated(at)[0], 1)

            dve.wait_ge(router_in, 32)
            dve.wait_ge(*read_out(("logits",)))
            step(nc.vector.tensor_tensor(biased[:, :, :], score[:, :, :], b_rt[:, :].unsqueeze(1).broadcast_to([P, G, N_EXP]), ALU.add))
            for g in range(G):
                step(nc.vector.max(top8[:, g, :], biased[:, g, :]))
                step(nc.vector.match_replace(left_over[:, g, :], top8[:, g, :], biased[:, g, :], -1e30))
            nc.vector.tensor_tensor(chosen[:, :, :], left_over[:, :, :], biased[:, :, :], ALU.not_equal).then_inc(chosen_ready, 1)
            dve.wait_ge(chosen_ready, 1)
            step(nc.vector.tensor_tensor(weight[:, :, :], score[:, :, :], chosen[:, :, :], ALU.mult))
            step(nc.vector.reduce_sum(total_w[:, :], weight[:, :, :], axis=AXX))
            step(nc.vector.tensor_scalar(total_w[:, :], total_w[:, :], 1e-20, None, ALU.add))
            step(nc.vector.reciprocal(total_w[:, :], total_w[:, :]))
            for g in range(G):
                step(nc.vector.tensor_scalar(weight[:, g, :], weight[:, g, :], total_w[:, g:g + 1], ROUTED_SCALE, ALU.mult, ALU.mult))

            def taken(use, ins):
                s, full = read_out(use)
                ins.then_inc(s, 1)
                dve.wait_ge(s, full)

            def awaited(use):
                dve.wait_ge(scratch_ready, SCRATCH_NO[use] + 1)
                return scratch(use)

            b = awaited(("place",))
            taken(("place",), nc.vector.scalar_tensor_tensor(
                place[:, :, :], b[:, 0:G * N_EXP].rearrange("p (g e) -> p g e", g=G), 1.0, chosen[:, :, :], ALU.add, ALU.mult))
            b = awaited(("count",))
            taken(("count",), nc.vector.tensor_copy(counts[0:N_EXP, :], b[0:N_EXP, 0:1]))
            step(nc.vector.tensor_scalar(has_chunk[0:N_EXP, :], con("chunk_at")[0:N_EXP, :], counts[0:N_EXP, :], None, ALU.is_lt))
            nc.vector.reduce_sum(n_chunks[0:N_EXP, :], has_chunk[0:N_EXP, :], axis=AXX).then_inc(counted, 1)
            b = awaited(("before",))
            step(nc.vector.tensor_scalar(first_item[:, :], con("chunk_no")[0:N_EXP, :], b[0:N_EXP, 0:1], None, ALU.add))
            taken(("before",), nc.vector.tensor_scalar(last_turn[0:1, 1:2], b[0:1, 1:2], -1.0, None, ALU.add))
            nc.vector.tensor_scalar(last_turn[0:1, 0:1], last_turn[0:1, 1:2], 2, None, ALU.logical_shift_right).then_inc(table_ready, 1)
            nc.vector.memset(of_item[:, :], 0.0)
            step(nc.vector.memset(at_item[:, :], 0.0))
            for ch in range(MAX_CHUNKS):
                step(nc.vector.tensor_scalar(is_item[:, :], con("item_no")[0:N_EXP, :], first_item[:, ch:ch + 1], has_chunk[0:N_EXP, ch:ch + 1], ALU.is_equal, ALU.mult))
                nc.vector.tensor_tensor(of_item[:, :], of_item[:, :], is_item[:, :], ALU.add)
                nc.vector.scalar_tensor_tensor(at_item[:, :], is_item[:, :], float(ch * SLOTS), at_item[:, :], ALU.mult, ALU.add).then_inc(listed, 1)
                dve.wait_ge(listed, ch + 1)
            b = awaited(("items",))
            nc.vector.tensor_copy(item_expert[0:1, :], b[0:1, 0:MAX_ITEMS]).then_inc(table_ready, 1)
            taken(("items",), nc.vector.tensor_copy(item_at[:, :], b[:, P:P + MAX_ITEMS]))
            b = awaited(("item_rows",))
            two = b[:, 0:2 * G * MAX_ITEMS].rearrange("p (a g i) -> p a g i", a=2, g=G)
            nc.vector.tensor_tensor(item_place[:, :, :], two[:, 0], item_at[:, :].unsqueeze(1).broadcast_to([P, G, MAX_ITEMS]), ALU.subtract)
            taken(("item_rows",), nc.vector.tensor_copy(item_weight[:, :, :], two[:, 1]))

            def low(j, c):
                p = 12 * j + c
                s = raw_slot((j, c))
                dve.wait_ge(piece_in[s], val(32 * (2 * j + c // RAW + 1)))
                dve.wait_ge(hi_ready, val(p + 1))
                if above_zero(p - N_SPLIT + 1):
                    dve.wait_ge(piece_used, val(p - N_SPLIT + 1))
                out, hi = (w[:, c % N_SPLIT, :].rearrange("p (k b n) -> p k b n", k=KD // 2, b=2) for w in (w_lo, w_hi))
                src = raw[:, s, :].rearrange("p (b k n) -> p k b n", k=KD // 2, b=2)
                nc.vector.tensor_tensor(out, src, hi.bitcast(F32), ALU.subtract).then_inc(low_up_ready, 1)

            def turned_out(n):
                dve.wait_ge(hid_hi_ready, val(n))
                nc.vector.tensor_tensor(hid_t[:, :, SLOTS:2 * SLOTS], turn_bank[:, 0:2 * SLOTS].rearrange("p (f s) -> p f s", f=2),
                                        hid_t[:, :, 0:SLOTS].bitcast(F32), ALU.subtract).then_inc(hid_lo_ready, 1)

            def y_low(m, h):
                dve.wait_ge(y_hi_ready, val(2 * m + h + 1))
                nc.vector.tensor_tensor(y_lo[:, h, :], y_bank[h][:, :], y_hi[:, h, :].bitcast(F32), ALU.subtract).then_inc(y_lo_ready, 1)

            def gu_sum(m):
                dve.wait_ge(gu_lo_ready, val(m + 1))
                need(silu_ready, m)
                need(hid_ready, m)
                nc.vector.tensor_tensor(gu[:, :], gu_bank[0:SLOTS, :], gu_lo[:, :], ALU.add).then_inc(gu_sum_ready, 1)

            def hidden(m, q):
                dve.wait_ge(silu_ready, val(m + 1))
                need(turned, m + 1)
                nc.vector.scalar_tensor_tensor(hid[:, :], silu_g[:, :], slot_gate[:, q:q + 1], gu[:, DE:2 * DE], ALU.mult, ALU.mult).then_inc(hid_ready, 1)

            def gather_out(j):
                for k in range(1, KD, 2):
                    dve.wait_ge(gathered, val((KD + 1) * j + k + 2))
                    nc.vector.tensor_copy(x_g[:, k], gather_bank[(k + 1) % 4][:, :].rearrange("p (q s) -> p q s", q=ITEMS_PER_TURN)).then_inc(x_odd_ready, 1)

            def picks(j):
                need(turned, j * ITEMS_PER_TURN)
                need(gathered, (KD + 1) * j)
                items = bass.ds(val(j * ITEMS_PER_TURN), ITEMS_PER_TURN)
                for g in range(G):
                    nc.vector.tensor_tensor(
                        pick[:, g], con("slot_no").unsqueeze(1).broadcast_to([P, ITEMS_PER_TURN, 2 * SLOTS]),
                        item_place[:, g, items].unsqueeze(2).broadcast_to([P, ITEMS_PER_TURN, 2 * SLOTS]),
                        ALU.is_equal)
                nc.vector.tensor_copy(gate4[:, :, :], item_weight[:, :, items]).then_inc(pick_ready, 1)

            def turn(j, first):
                for q in range(ITEMS_PER_TURN):
                    n = j * ITEMS_PER_TURN + q
                    start = first and q == 0
                    low(j, 3 * q - 1 + start)
                    if not start:
                        gu_sum(n - 1)
                        if not (first and q == 1):
                            turned_out(n - 1)
                        hidden(n - 1, (q - 1) % ITEMS_PER_TURN)
                    if q:
                        low(j, 3 * q + start)
                    else:
                        picks(j)
                    if not (first and q < 2):
                        for h in range(2):
                            y_low(n - 2, h)
                    if q == 0:
                        gather_out(j)
                        low(j, 3 * q + start)

            more_turns = turns_after_first(dve)
            turn(0, True)
            with dve.Fori(0, more_turns) as t:
                turn(Count(t, 1, 1), False)
            turns = Count(more_turns, 1, 1)
            n_items = turns * ITEMS_PER_TURN
            gu_sum(n_items - 1)
            turned_out(n_items - 1)
            hidden(n_items - 1, ITEMS_PER_TURN - 1)
            for h in range(2):
                y_low(n_items - 2, h)
            turned_out(n_items)
            for h in range(2):
                y_low(n_items - 1, h)

            dve.wait_ge(moe_done, 1)
            dve.wait_ge(ln2_in, 32)
            dve.wait_ge(mod_in[5], 32)
            for g in range(G):
                for h in range(2):
                    cols = slice(h * BANK, (h + 1) * BANK)
                    step(nc.vector.tensor_tensor(gate2[:, g, cols], acc_bank[2 * g + h][:, :], gate2[:, g, cols], ALU.mult))
                step(nc.vector.scalar_tensor_tensor(resid[:, g, :], resid[:, g, :], ALPHA, gate2[:, g, :], ALU.mult, ALU.add))
                normalize(resid[:, g, :], resid[:, g, :])
                step(nc.vector.tensor_tensor(resid[:, g, :], resid[:, g, :], ln2_rows[0][:, :], ALU.mult))
                nc.vector.tensor_tensor(resid[:, g, :], resid[:, g, :], ln2_rows[1][:, :], ALU.add).then_inc(out_ready, 1)

        @block.tensor
        def _(pe):
            mm = nc.tensor.matmul

            def need(s, value):
                if above_zero(value):
                    pe.wait_ge(s, val(value))

            def bank_for(product):
                n = PRODUCT_NO[product]
                if n >= N_ROT:
                    pe.wait_ge(bank_free[n % N_ROT], n // N_ROT)
                return rotating(product)

            def scratch_for(use):
                n = SCRATCH_NO[use]
                if n >= 2:
                    pe.wait_ge(scratch_free[n % 2], n // 2)
                return scratch(use)

            def arrived(chunk):
                slot, full = chunk_arrived(chunk)
                pe.wait_ge(ring_in[slot], full)
                return ring[:, slot, :]

            def modulation(c):
                out = bank_for(("ada", c))
                w = arrived(("ada", c)).rearrange("p (k n) -> p k n", k=KD)
                for k in range(KD):
                    ins = mm(out[0:G, :], cond_s[:, k, :], w[:, k, :], start=k == 0, stop=k == KD - 1)
                ins.then_inc(product_ready, 1)
                nc.tensor.drain().then_inc(chunk_used, 1)

            def turn_tiles(use, tiles_in):
                out = scratch_for(use)
                for i, t in enumerate(tiles_in):
                    ins = nc.tensor.transpose(out[0:t.free_size(), i * P:i * P + t.partition_size()], t, ident)
                ins.then_inc(scratch_ready, 1)

            def w_in_product(at):
                _, c, h = at
                out = bank_for(at)
                w = arrived(("in", c)).rearrange("p (k n) -> p k n", k=KD)
                halves = out[:, :].rearrange("p (a t) -> p a t", a=2)
                if c in (2, 3, 0, 6) or at == ("in", 5, 1):
                    for a in range(2):
                        ct = 2 + a if c == 5 else 2 * h + a
                        for k in range(KD):
                            ins = mm(halves[:, a], w[:, k, ct * P:(ct + 1) * P], h_t[:, k, :], start=k == 0, stop=k == KD - 1)
                elif c == 5:
                    for g in range(G):
                        for k in range(KD):
                            ins = mm(halves[:, g], h_t[:, k, tok(g)], w[:, k, 0:FW], start=k == 0, stop=k == KD - 1)
                else:
                    for k in range(KD):
                        ins = mm(out[:, :], h_t[:, k, tok(h)], w[:, k, :], start=k == 0, stop=k == KD - 1)
                ins.then_inc(product_ready, 1)
                if h == 1:
                    nc.tensor.drain().then_inc(chunk_used, 1)

            def scan_scores(s):
                d, g, n = STEPS[s]
                out = scratch_for(("step", s))
                if d is None:
                    pe.wait_ge(key_sum_ready, g + 1)
                else:
                    pe.wait_ge(q_ready, s + 1)
                    pe.wait_ge(k_ready, s + 1)
                for h in range(HEADS):
                    query = q_t[:, h, tok(g)] if d is None else lev_q[:, s % 2, h, :]
                    ins = mm(out[:, h * P:(h + 1) * P], lev_k[:, s % 2, h, :], query, start=True, stop=True)
                ins.then_inc(scratch_ready, 1)

            pe.wait_ge(cond_ready, 1)
            for c in ADA_EARLY:
                modulation(c)
            pe.wait_ge(cst_in, 16)
            for g in range(G):
                pe.wait_ge(norm_ready, g + 1)
                for a in range(2):
                    turn_tiles(("h", g, a), [h_tok[:, g, k * P:(k + 1) * P] for k in range(4 * a, 4 * a + 4)])
            for g in range(G):
                for a in range(2):
                    pe.wait_ge(*read_out(("h", g, a)))
            for what, at in schedule():
                if what == "step":
                    scan_scores(at)
                elif at[0] == "ada":
                    modulation(at[1])
                else:
                    w_in_product(at)

            for g in range(G):
                out = scratch_for(("four1", g))
                for ct in range(2):
                    ins = mm(out[:, ct * 2 * P:(ct + 1) * 2 * P], four[:, g, ct * P:(ct + 1) * P], dft[:, 0:2 * P], start=True, stop=True)
                ins.then_inc(scratch_ready, 1)
            for g in range(G):
                pe.wait_ge(*read_out(("step", 2 * G * len(LEVELS) + g)))
                if g == 1:
                    pe.wait_ge(start_q_ready, 2)
                for h in range(HEADS):
                    out = o_bank[g][:, h * DK:(h + 1) * DK]
                    v = value[:, g, h * DK:(h + 1) * DK]
                    ins = mm(out, scores[:, g, h, :], v, start=True, stop=g == 0)
                    if g == 1:
                        for d in range(2):
                            ins = mm(out, lev_q[:, d, h, :], state_in[:, d, h, :], start=False, stop=d == 1)
                ins.then_inc(o_ready, 1)
            for d in range(2):
                pe.wait_ge(end_key_ready, d + 1)
                turn_tiles(("ends", d), [kd_sb[:, d, h, :] for h in range(HEADS)])
            for d in range(2):
                pe.wait_ge(*read_out(("ends", d)))
                out = scratch_for(("state", d))
                for h in range(HEADS):
                    ins = mm(out[:, h * DK:(h + 1) * DK], kd_t[:, d, h, :], value[:, 0, h * DK:(h + 1) * DK], start=True, stop=True)
                ins.then_inc(scratch_ready, 1)
            for g in range(G):
                pe.wait_ge(*read_out(("four1", g)))
            out = scratch_for(("four2",))
            for ct in range(2):
                for g in range(G):
                    at = out[:, ct * TOK + g * P:ct * TOK + (g + 1) * P]
                    mm(at, dft[:, 2 * P:3 * P], four_f[:, g, ct, 0:P], start=True, stop=False)
                    ins = mm(at, dft[:, 3 * P:4 * P], four_f[:, g, ct, P:2 * P], start=False, stop=True)
            ins.then_inc(scratch_ready, 1)
            for g in range(G):
                pe.wait_ge(a_ready, g + 1)
                turn_tiles(("a", g), [o_sb[:, h, :] for h in range(HEADS)])
            pe.wait_ge(*read_out(("four2",)))
            pe.wait_ge(conv_ready, 1)
            w_a = arrived(("proj_hgrn", 0)).rearrange("p (k n) -> p k n", k=HEADS)
            w_fc = arrived(("proj_fc", 0)).rearrange("p (b k n) -> p b k n", b=2, k=2)
            for g in range(G):
                pe.wait_ge(*read_out(("a", g)))
                for h in range(2):
                    cols = slice(h * BANK, (h + 1) * BANK)
                    for b in range(NB):
                        out = bank_for(("proj", g, h, b))
                        left = (a_t, f_t, c_t)[b]
                        right = (w_a, w_fc[:, 0], w_fc[:, 1])[b]
                        n_k = HEADS if b == 0 else 2
                        for k in range(n_k):
                            ins = mm(out[:, :], left[:, k, tok(g)], right[:, k, cols], start=k == 0, stop=k == n_k - 1)
                        ins.then_inc(product_ready, 1)
            nc.tensor.drain().then_inc(chunk_used, 2)
            for g in range(G):
                for a in range(2):
                    pe.wait_ge(merged_ready, 2 * g + a + 1)
                    turn_tiles(("merged", g, a), [merged[:, g, k * P:(k + 1) * P] for k in range(4 * a, 4 * a + 4)])
            for g in range(G):
                for a in range(2):
                    pe.wait_ge(*read_out(("merged", g, a)))
            for h in range(2):
                w = arrived(("out", h)).rearrange("p (k n) -> p k n", k=KD)
                for g in range(G):
                    out = bank_for(("out", h, g))
                    for k in range(KD):
                        ins = mm(out[:, :], h_t[:, k, tok(g)], w[:, k, :], start=k == 0, stop=k == KD - 1)
                    ins.then_inc(product_ready, 1)
                nc.tensor.drain().then_inc(chunk_used, 1)
            nc.tensor.drain().then_inc(mixer_done, 1)

            for g in range(G):
                pe.wait_ge(norm_ready, G + g + 1)
                for a in range(2):
                    turn_tiles(("h2", g, a), [h2_tok[:, g, :].rearrange("p (q k) -> p k q", k=KD)[:, k] for k in range(4 * a, 4 * a + 4)])
            for g in range(G):
                for a in range(2):
                    pe.wait_ge(*read_out(("h2", g, a)))
            pe.wait_ge(router_in, 32)
            out = scratch_for(("logits",))
            for g in range(G):
                for k in range(KD):
                    ins = mm(out[:, g * N_EXP:(g + 1) * N_EXP], h_t[:, k, tok(g)], w_rt[:, k, :], start=k == 0, stop=k == KD - 1)
            ins.then_inc(scratch_ready, 1)
            w = arrived(("shared_up", 0)).rearrange("p (b k n) -> p b k n", b=2, k=KD)
            for f in range(2):
                out = bank_for(("shared", f))
                for b in range(2):
                    for k in range(KD):
                        ins = mm(out[:, b * TOK:(b + 1) * TOK], w[:, b, k, f * P:(f + 1) * P], h_t[:, k, :], start=k == 0, stop=k == KD - 1)
                ins.then_inc(product_ready, 1)
            nc.tensor.drain().then_inc(chunk_used, 1)
            for f in range(2):
                pe.wait_ge(*evacuated(("shared", f)))
            for g in range(G):
                pe.wait_ge(a_ready, g + 1)
            for at in [("out", 1, g) for g in range(G)]:
                pe.wait_ge(*evacuated(at))
            w = arrived(("shared_down", 0))[:, 0:2 * D].rearrange("p (k n) -> p k n", k=2)
            for g in range(G):
                for h in range(2):
                    for f in range(2):
                        ins = mm(acc_bank[2 * g + h][:, :], hid_sh[:, f, tok(g)], w[:, f, h * BANK:(h + 1) * BANK], start=f == 0, stop=f == 1)
            nc.tensor.drain().then_inc(chunk_used, 1)

            pe.wait_ge(chosen_ready, 1)
            out = scratch_for(("place",))
            mm(out[:, 0:N_EXP], before, chosen[:, 0, :], start=True, stop=True)
            mm(out[:, N_EXP:2 * N_EXP], ones, chosen[:, 0, :], start=True, stop=False)
            mm(out[:, N_EXP:2 * N_EXP], before, chosen[:, 1, :], start=False, stop=True).then_inc(scratch_ready, 1)
            out = scratch_for(("count",))
            for g in range(G):
                ins = mm(out[0:N_EXP, 0:1], chosen[:, g, :], ones[:, 0:1], start=g == 0, stop=g == G - 1)
            ins.then_inc(scratch_ready, 1)
            pe.wait_ge(counted, 1)
            out = scratch_for(("before",))
            mm(out[0:N_EXP, 0:1], before[0:N_EXP, 0:N_EXP], n_chunks[0:N_EXP, :], start=True, stop=True)
            mm(out[0:1, 1:2], n_chunks[0:N_EXP, :], ones[0:N_EXP, 0:1], start=True, stop=True).then_inc(scratch_ready, 1)
            out = scratch_for(("rows",))
            for i, t in enumerate([place[:, 0, :], place[:, 1, :], weight[:, 0, :], weight[:, 1, :]]):
                ins = nc.tensor.transpose(out[0:N_EXP, i * P:(i + 1) * P], t, ident)
            ins.then_inc(scratch_ready, 1)
            pe.wait_ge(listed, MAX_CHUNKS)
            out = scratch_for(("items",))
            mm(out[0:1, 0:MAX_ITEMS], con("part_no")[0:N_EXP, :], of_item[:, :], start=True, stop=True)
            mm(out[:, P:P + MAX_ITEMS], ones[0:N_EXP, :], at_item[:, :], start=True, stop=True).then_inc(scratch_ready, 1)
            pe.wait_ge(*read_out(("rows",)))
            out = scratch_for(("item_rows",))
            for a in range(2):
                for g in range(G):
                    i = (a * G + g) * MAX_ITEMS
                    ins = mm(out[:, i:i + MAX_ITEMS], rows_t[:, a, g, :], of_item[:, :], start=True, stop=True)
            ins.then_inc(scratch_ready, 1)
            pe.wait_ge(*read_out(("items",)))
            pe.wait_ge(*read_out(("item_rows",)))
            nc.tensor.drain().then_inc(split_free, 1)

            pe.wait_ge(split_ready, G)
            pe.wait_ge(h_lo_ready, G)

            def gather(j):
                n = j * ITEMS_PER_TURN
                pe.wait_ge(pick_ready, val(j + 1))
                for u in range(KD + 1):
                    out = gather_bank[u % 4]
                    if u == 0:
                        need(gu_sum_ready, n)
                        need(gu_lo_ready, n)
                    elif u == 1:
                        need(put_back_ready, n)
                        need(hid_hi_ready, n - 1)
                        need(hid_lo_ready, n - 1)
                    elif u in (2, 3):
                        need(y_hi_ready, 2 * (n - 1))
                        need(y_lo_ready, 2 * (n - 1))
                    elif u == 4:
                        pe.wait_ge(slot_gate_ready, val(j + 1))
                    elif u % 2:
                        pe.wait_ge(x_even_ready, val(KD // 2 * j + (u - 5) // 2 + 1))
                    else:
                        pe.wait_ge(x_odd_ready, val(KD // 2 * j + (u - 5) // 2 + 1))
                    if u == 0:
                        for q in range(ITEMS_PER_TURN):
                            for g in range(G):
                                ins = mm(out[0:SLOTS, q:q + 1], pick[:, g, q, 0:SLOTS].bitcast(F32), gate4[:, g, q:q + 1], start=g == 0, stop=g == G - 1)
                    else:
                        by_item = out[:, :].rearrange("p (q b s) -> p q b s", q=ITEMS_PER_TURN, b=2)
                        for b, part in enumerate((h_hi, h_lo)):
                            for g in range(G):
                                ins = mm(by_item[:, :, b, :], part[:, g, u - 1, :], pick[:, g, :, 0:SLOTS], start=g == 0, stop=g == G - 1)
                    ins.then_inc(gathered, 1)

            def up(j, c, a, q):
                s = c % N_SPLIT
                pe.wait_ge(low_up_ready, val(2 * (j * ITEMS_PER_TURN + q) + a + 1))
                for k in range(KD // 2):
                    for b, w in enumerate((w_hi, w_lo)):
                        ins = mm(gu_bank[:, :], x_g[:, a * KD // 2 + k, q, :], w[:, s, k * BANK:(k + 1) * BANK],
                                 start=a == k == b == 0, stop=a == b == 1 and k == KD // 2 - 1)
                ins.then_inc(piece_used, 1)

            def turn_over(n, hidden, q):
                if hidden:
                    pe.wait_ge(hid_ready, val(n))
                need(put_back_ready, n)
                need(hid_hi_ready, n - 1)
                need(hid_lo_ready, n - 1)
                if q is None:
                    scatter(n - 2, ITEMS_PER_TURN - 2)
                else:
                    for g in range(G):
                        ins = nc.tensor.transpose(turn_bank[:, (1 + g) * P:(2 + g) * P], pick[:, g, q, :].bitcast(F32), ident)
                if hidden:
                    for f in range(2):
                        ins = nc.tensor.transpose(turn_bank[:, f * SLOTS:(f + 1) * SLOTS], hid[:, f::2], ident[0:SLOTS, 0:SLOTS])
                ins.then_inc(turned, 1)

            def scatter(m, q):
                pe.wait_ge(put_back_ready, val(m + 1))
                pe.wait_ge(y_lo_ready, val(2 * m + 2))
                for g in range(G):
                    for h in range(2):
                        for y in (y_hi, y_lo):
                            ins = mm(acc_bank[2 * g + h][:, :], put_back[:, q, g, :], y[:, h, :], start=False, stop=True, skip_group_check=True)
                ins.then_inc(scattered, 1)

            def down(c, m):
                s = c % N_SPLIT
                pe.wait_ge(low_down_ready, val(m + 1))
                pe.wait_ge(hid_lo_ready, val(m + 1))
                need(y_lo_ready, 2 * m)
                for h in range(2):
                    for f in range(2):
                        for b, w in enumerate((w_hi, w_lo)):
                            ins = mm(y_bank[h][:, :], hid_t[:, f, :], w[:, s, f * D + h * BANK:f * D + (h + 1) * BANK],
                                     start=f == b == 0, stop=f == b == 1)
                    ins.then_inc(piece_used if h else y0_ready, 1)

            def turn(j, first):
                gather(j)
                pe.wait_ge(x_even_ready, val(KD // 2 * (j + 1)))
                pe.wait_ge(x_odd_ready, val(KD // 2 * (j + 1)))
                for q in range(ITEMS_PER_TURN):
                    n = j * ITEMS_PER_TURN + q
                    start = first and q == 0
                    need(gu_sum_ready, n)
                    up(j, 3 * q - 1 + start, 0, q)
                    up(j, 3 * q + start, 1, q)
                    turn_over(n, not start, q)
                    if not (first and q < 2):
                        scatter(n - 2, (q - 2) % ITEMS_PER_TURN)
                    if not start:
                        down(3 * q + 1, n - 1)

            more_turns = turns_after_first(pe)
            turn(0, True)
            with pe.Fori(0, more_turns) as t:
                turn(Count(t, 1, 1), False)
            turns = Count(more_turns, 1, 1)
            n_items = turns * ITEMS_PER_TURN
            turn_over(n_items, True, None)
            down(-1, n_items - 1)
            scatter(n_items - 1, ITEMS_PER_TURN - 1)
            nc.tensor.drain().then_inc(moe_done, 1)


_INS = ['x_prompt', 'x_sample', 'c', 'state_hgrn', 'c_ctx', 'w_ada', 'b_ada', 'w_in', 'b_gate', 'hgrn_lb', 'hgrn_norm',
        'conv_w', 'w_proj_hgrn', 'w_proj_fourier', 'w_proj_conv', 'w_out', 'ln1_g', 'ln1_b', 'ln2_g', 'ln2_b',
        'w_router', 'b_router', 'w_exp_gate', 'w_exp_up', 'w_exp_down', 'w_sh_gate', 'w_sh_up', 'w_sh_down']
_OUTS = [("y_prompt_out", (1, P, D)), ("y_sample_out", (1, P, D)), ("state_out_dram", (1, 1, 2, HEADS, DK, DK))]


def kernel(**inputs):
    import concourse.bacc as bacc
    from concourse.bass_utils import run_bass_kernel_spmd

    nc = bacc.Bacc("TRN2", target_bir_lowering=False, num_devices=1)
    arrays = {f"in_{name}": np.ascontiguousarray(inputs[name]) for name in _INS}
    arrays |= {"shape_table": CST, "shape_masks": MASKS, "shape_pos": POS}
    args = [nc.dram_tensor(n, a.shape, mybir.dt.from_np(a.dtype), kind="ExternalInput").ap() for n, a in arrays.items()]
    args += [nc.dram_tensor(n, shape, F32, kind="ExternalOutput").ap() for n, shape in _OUTS]
    hybrid_layer(nc, *args)
    r = run_bass_kernel_spmd(nc, [arrays], core_ids=[0])
    return tuple(r.results[0][n] for n, _ in _OUTS)
```

```python
from contextlib import ExitStack

import numpy as np

import concourse.bass as bass
from concourse import mybir
from concourse.alu_op_type import AluOpType as ALU

F32 = mybir.dt.float32
F32R = mybir.dt.float32r
I32 = mybir.dt.int32
U8 = mybir.dt.uint8
ACT = mybir.ActivationFunctionType
AXX = mybir.AxisListType.X

P = 128
D = 1024
KD = D // P
G = 2
TOK = G * P
HEADS, DK = 4, 128
HW = HEADS * DK
FGD = 64
FW = 256
CW = 256
NB = 3
N_EXP, TOP_K, DE = 64, 8, 256
ROUTED_SCALE = 2.5
ALPHA = 2 ** 0.25
LN_EPS = 1e-6
RMS_EPS = 1e-6
F_MIN = 1e-30
LN_SPLIT = 2.0 ** -60
BANK = 512
COL_GROUPS, COLS = 4, 32

LEVELS = [64, 32, 16, 8, 4, 2, 1]
N_MASK = 2 * len(LEVELS) + 1
SLOTS = 64
MAX_CHUNKS = TOK // SLOTS
MAX_ITEMS = 96
ITEMS_PER_TURN = 4
ACT_TILES, DVE_TILES = [0, 2, 4, 6, 7], [1, 3, 5]

CST_COLS = {}


def shape_constants():
    parts = []

    def put(name, a):
        at = sum(x.shape[1] for x in parts)
        CST_COLS[name] = (at, at + a.shape[1])
        full = np.zeros((P, a.shape[1]), np.float32)
        full[:a.shape[0]] = a
        parts.append(full)

    i = np.arange(P)
    put("ident", np.eye(P))
    put("ones", np.ones((P, P)))
    put("before", (i[:, None] < i[None, :]))
    put("row_sum", i[:, None] % COLS == np.arange(2)[None])
    put("slot_no", np.tile(np.arange(SLOTS) + 1.0, 2)[None].repeat(P, 0))
    put("item_no", np.arange(MAX_ITEMS)[None].repeat(P, 0))
    put("chunk_no", np.arange(MAX_CHUNKS)[None].repeat(P, 0))
    put("chunk_at", (np.arange(MAX_CHUNKS) * SLOTS)[None].repeat(P, 0))
    put("part_no", i[:, None])
    keep = sum(x.shape[1] for x in parts)
    scale = 1.0 / np.sqrt(P * FGD)
    angle = 2 * np.pi * ((i[:, None] * i[None, :]) % P) / P
    put("dft_t", np.concatenate([np.cos(angle), np.sin(angle)], 1) * scale)
    c = np.arange(FGD)
    angle = 2 * np.pi * ((c[:, None] * c[None, :]) % FGD) / FGD
    put("dft_c", np.concatenate([np.kron(np.eye(P // FGD), np.cos(angle)),
                                 np.kron(np.eye(P // FGD), -np.sin(angle))], 1))
    table = np.concatenate(parts, 1).astype(np.float32)

    masks = np.zeros((P, N_MASK, P), np.float32)
    for direction in range(2):
        for n, half in enumerate(LEVELS):
            same = (i[:, None] // (2 * half)) == (i[None, :] // (2 * half))
            s_late = (i[:, None] // half) % 2 == 1
            t_late = (i[None, :] // half) % 2 == 1
            pick = same & ~s_late & t_late if direction == 0 else same & s_late & ~t_late
            masks[:, direction * len(LEVELS) + n] = pick
    masks[:, -1] = np.eye(P)

    quarter = D // 4
    omega = (1.0 / (10000.0 ** (np.arange(quarter, dtype=np.float32) / np.float32(quarter)))).astype(np.float32)
    row, col = (i // 64).astype(np.float32), (i % 64).astype(np.float32)
    ar, ac = row[:, None] * omega, col[:, None] * omega
    pos = np.concatenate([np.sin(ar), np.cos(ar), np.sin(ac), np.cos(ac)], -1).astype(np.float32)
    return table, keep, masks.reshape(P, N_MASK * P), pos


CST, CST_KEEP, MASKS, POS = shape_constants()

RING = 3
CH_BYTES = KD * BANK
ADA_EARLY = [0, 1, 2, 3]
ADA_LATE = [4, 5, 6, 7, 8, 9]
ADA_LAST = [10, 11]
ADA_ROWS = ADA_LATE + ADA_LAST
IN_ORDER = [2, 3, 0, 1, 4, 5, 6, 7, 8, 9, 10, 11, 12]
MIDDLE = ([("in", c) for c in IN_ORDER[:6]]
          + [chunk for c, a in zip(IN_ORDER[6:12], ADA_LATE) for chunk in (("in", c), ("ada", a))]
          + [("in", c) for c in IN_ORDER[12:]])
CHUNKS = ([("ada", c) for c in ADA_EARLY] + MIDDLE
          + [("proj_hgrn", 0), ("proj_fc", 0), ("out", 0), ("out", 1)] + [("ada", c) for c in ADA_LAST]
          + [("shared_up", 0), ("shared_down", 0)])
CHUNK_NO = {c: n for n, c in enumerate(CHUNKS)}
CHUNK_DMAS = {"ada": 1, "in": 1, "proj_hgrn": 1, "proj_fc": 2, "out": 1, "shared_up": 2, "shared_down": 1}


def chunk_arrived(chunk):
    n = CHUNK_NO[chunk]
    return n % RING, 16 * sum(CHUNK_DMAS[CHUNKS[m][0]] for m in range(n % RING, n + 1, RING))


RAW = 2 * RING


def raw_slot(p):
    return (p[1] + 2) % RAW


BRANCH_ORDER = [1, 2, 0]

PRODUCTS = ([("ada", c) for c in ADA_EARLY]
            + [p for kind, c in MIDDLE for p in ([("in", c, 0), ("in", c, 1)] if kind == "in" else [("ada", c)])]
            + [("proj", g, h, b) for g in range(G) for h in range(2) for b in BRANCH_ORDER]
            + [("out", h, g) for h in range(2) for g in range(G)]
            + [("ada", c) for c in ADA_LAST]
            + [("shared", f) for f in range(2)])
PRODUCT_NO = {p: n for n, p in enumerate(PRODUCTS)}
N_ROT = 3

class Count:

    def __init__(self, register, scale, more):
        self.register, self.scale, self.more = register, scale, more

    def __add__(self, k):
        return Count(self.register, self.scale, self.more + k)

    def __sub__(self, k):
        return self + -k

    def __mul__(self, k):
        return Count(self.register, k * self.scale, k * self.more)

    __rmul__ = __mul__

    def value(self):
        assert self.more > 0
        return self.register * self.scale + self.more


def val(n):
    return n.value() if isinstance(n, Count) else n


def above_zero(n):
    return isinstance(n, Count) or n > 0


STEPS = [(d, g, n) for d in range(2) for g in range(G) for n in range(len(LEVELS))] + \
        [(None, g, None) for g in range(G)]
SCRATCH = ([("mod", c) for c in ADA_EARLY] + [("h", g, a) for g in range(G) for a in range(2)]
           + [("step", s) for s in range(len(STEPS))]
           + [("four1", g) for g in range(G)]
           + [("ends", d) for d in range(2)] + [("state", d) for d in range(2)]
           + [("four2",)] + [("a", g) for g in range(G)]
           + [("merged", g, a) for g in range(G) for a in range(2)]
           + [("h2", g, a) for g in range(G) for a in range(2)]
           + [("logits",), ("place",), ("count",), ("before",), ("rows",), ("items",), ("item_rows",)])
SCRATCH_NO = {u: n for n, u in enumerate(SCRATCH)}
STAGES = ["scan output", "final keys", "final states", "fourier", "turn scan output"]
STEP_FROM = PRODUCT_NO[("in", 4, 0)]


def schedule(steps_first):
    left, stages = list(range(len(STEPS))), list(STAGES)
    for n in range(PRODUCT_NO[("in", IN_ORDER[0], 0)], PRODUCT_NO[("in", IN_ORDER[-1], 1)] + 1):
        between = []
        if n >= STEP_FROM and left and PRODUCTS[n][0] == "in":
            between = [("step", s) for s in left[:2]]
            left = left[2:]
        elif not left and stages:
            between = [("stage", stages.pop(0))]
        product = [("product", PRODUCTS[n])]
        yield from between + product if steps_first else product + between
    assert not left
    for name in stages:
        yield "stage", name


def hybrid_layer(nc, x_prompt, x_sample, c, state_hgrn, c_ctx, w_ada, b_ada, w_in, b_gate, hgrn_lb, hgrn_norm,
                 conv_w, w_proj_hgrn, w_proj_fourier, w_proj_conv, w_out, ln1_g, ln1_b, ln2_g, ln2_b, w_router,
                 b_router, w_exp_gate, w_exp_up, w_exp_down, w_sh_gate, w_sh_up, w_sh_down,
                 table, masks, pos, y_prompt, y_sample, state_new):
    ctx = ExitStack()
    with ctx:
        def sem(name):
            return ctx.enter_context(nc.semaphore(name))

        mixer_sbuf, experts_sbuf = ExitStack(), ExitStack()

        def keep(name, shape, dt=F32):
            return ctx.enter_context(nc.sbuf_tensor(name, shape, dt))

        def mix(name, shape, dt=F32):
            return mixer_sbuf.enter_context(nc.sbuf_tensor(name, shape, dt))

        def moe(name, shape, dt=F32):
            return experts_sbuf.enter_context(nc.sbuf_tensor(name, shape, dt))

        ring = keep("ring", [P, RING, CH_BYTES])
        cst = keep("cst", [P, CST_KEEP])
        resid = keep("resid", [P, G, D])
        gate2 = keep("gate2", [P, G, D])
        bn = keep("bn", [P, 2, 6])
        mv = keep("mv", [P, 2])
        vareps = keep("vareps", [P, 1])
        std = keep("std", [P, 1])
        rstd = keep("rstd", [P, 1])
        counts = keep("counts", [P, 1])
        has_chunk = keep("has_chunk", [P, MAX_CHUNKS])
        n_chunks = keep("n_chunks", [P, 1])
        item_expert = keep("item_expert", [1, MAX_ITEMS], I32)
        last_turn = keep("last_turn", [1, 2], I32)

        def con(name):
            a, b = CST_COLS[name]
            return cst[:, a:b]

        ident, ones, before = con("ident"), con("ones"), con("before")

        dft = mix("dft", [P, table.shape[1] - CST_KEEP])
        mask_sb = mix("mask_sb", [P, N_MASK, P], U8)
        cond_t = mix("cond_t", [P, G, KD])
        cond_s = mix("cond_s", [P, KD, G])
        b_ada_t = mix("b_ada_t", [P, 2 * KD])
        mod_t = mix("mod_t", [P, 2, KD, G])
        mod_row = mix("mod_row", [G, 2, BANK])
        b_ada_sb = mix("b_ada_sb", [G, 2, BANK])
        mod_a = mix("mod_a", [P, G, D])
        mod_b = mix("mod_b", [P, G, D])
        h_t = mix("h_t", [P, KD, TOK])
        gates = mix("gates", [P, G, NB, D])
        fgate = mix("fgate", [P, 2, HEADS, TOK])
        kgate = mix("kgate", [P, 2, HEADS, TOK])
        decay = mix("decay", [P, 2, HEADS, TOK])
        q_t = mix("q_t", [P, HEADS, TOK])
        tmp = mix("tmp", [P, HEADS, TOK])
        lb_in = mix("lb_in", [P, 2 * HEADS])
        lb = mix("lb", [P, 2 * HEADS])
        lb_e = mix("lb_e", [P, 2 * HEADS])
        lb_one = mix("lb_one", [P, 2 * HEADS])
        value = mix("value", [P, G, HW])
        out_gate = mix("out_gate", [P, G, HW])
        norm_row = mix("norm_row", [P, HW])
        four = mix("four", [P, G, FW])
        four_f = mix("four_f", [P, G, 2, 2 * P])
        conv_b = mix("conv_b", [P, 2, TOK])
        conv_c = mix("conv_c", [P, 2, TOK])
        conv_h = mix("conv_h", [P, 2, TOK])
        conv_z = mix("conv_z", [P, 2, G, P + 2])
        conv_wt = mix("conv_wt", [P, 2, 3])
        b_gate_sb = mix("b_gate_sb", [P, BANK])
        lev_e = mix("lev_e", [P, 2, HEADS, P])
        lev_q = mix("lev_q", [P, 2, HEADS, P])
        lev_k = mix("lev_k", [P, 2, HEADS, P])
        scores = mix("scores", [P, G, HEADS, P])
        o_ss = mix("o_ss", [P, HEADS])
        o_r = mix("o_r", [P, HEADS])
        scan_end = mix("scan_end", [P, HEADS, G])
        state_in = mix("state_in", [P, 2, HEADS, DK])
        cond_pad = lev_q[:, 0, 0:2, :].rearrange("p h t -> p (h t)").rearrange("p (k c) -> p k c", k=KD)
        mod_part = lev_e[:, :, :, :].rearrange("p a h t -> p a (h t)")
        h_tok = gates[:, 0, 0:2, :]
        pos_sb = gates[:, 0, 2, :]
        mask_in = gates[:, 1, :, :].rearrange("p b d -> p (b d)")[:, 0:N_MASK * P]
        merged = decay[:, :, :, :].rearrange("p a h t -> p (a h t)").rearrange("p (g d) -> p g d", g=G)
        a_t = q_t
        f_t = conv_c
        c_t = conv_h
        state_out = kgate[:, 0, :, :].rearrange("p h t -> p (h t)").rearrange("p (d h v) -> p d h v", d=2, h=HEADS)
        kd_sb = lev_k
        kd_t = lev_e
        scale2 = gates[:, 0, 0:2, :]
        h2_tok = gates[:, 1, 0:2, :]
        ln1_rows = [gates[:, 0, 2, :], gates[:, 1, 2, :]]
        wide_tmp = tmp[:, :, :].rearrange("p h t -> p (h t)")
        mod_dram = nc.dram_tensor("mod_dram", [G, 4 * D], F32).ap()
        mixer_sbuf.close()

        raw = ring[:, :, :].rearrange("p r n -> p (r n)").rearrange("p (s n) -> p s n", s=RAW)
        PIECE = 2 * D
        N_SPLIT = 4
        w_hi = moe("w_hi", [P, N_SPLIT, PIECE], F32R)
        w_lo = moe("w_lo", [P, N_SPLIT, PIECE], F32R)
        h_hi = moe("h_hi", [P, G, KD, P], F32R)
        h_lo = moe("h_lo", [P, G, KD, P], F32R)
        x_g = moe("x_g", [P, KD, ITEMS_PER_TURN, 2 * SLOTS], F32R)
        pick = moe("pick", [P, G, ITEMS_PER_TURN, 2 * SLOTS], F32R)
        gate4 = moe("gate4", [P, G, ITEMS_PER_TURN])
        slot_gate = moe("slot_gate", [SLOTS, ITEMS_PER_TURN])
        put_back = moe("put_back", [P, ITEMS_PER_TURN, G, P], F32R)
        gu_lo = moe("gu_lo", [SLOTS, 2 * DE])
        gu = moe("gu", [SLOTS, 2 * DE])
        silu_g = moe("silu_g", [SLOTS, DE])
        hid = moe("hid", [SLOTS, DE])
        hid_t = moe("hid_t", [P, 2, 2 * SLOTS], F32R)
        y_hi = moe("y_hi", [P, 2, BANK], F32R)
        y_lo = moe("y_lo", [P, 2, BANK], F32R)
        hid_sh = moe("hid_sh", [P, 2, TOK])
        silu_sh = moe("silu_sh", [P, TOK])
        w_rt = moe("w_rt", [P, KD, N_EXP])
        b_rt = moe("b_rt", [P, N_EXP])
        score = moe("score", [P, G, N_EXP])
        biased = moe("biased", [P, G, N_EXP])
        left_over = moe("left_over", [P, G, N_EXP])
        top8 = moe("top8", [P, G, TOP_K])
        chosen = moe("chosen", [P, G, N_EXP])
        weight = moe("weight", [P, G, N_EXP])
        total_w = moe("total_w", [P, G])
        place = moe("place", [P, G, N_EXP])
        rows_t = moe("rows_t", [N_EXP, 2, G, P])
        first_item = moe("first_item", [N_EXP, MAX_CHUNKS])
        is_item = moe("is_item", [N_EXP, MAX_ITEMS])
        of_item = moe("of_item", [N_EXP, MAX_ITEMS])
        at_item = moe("at_item", [N_EXP, MAX_ITEMS])
        item_at = moe("item_at", [P, MAX_ITEMS])
        item_place = moe("item_place", [P, G, MAX_ITEMS])
        item_weight = moe("item_weight", [P, G, MAX_ITEMS])
        ln2_rows = [moe("ln2_g_row", [P, D]), moe("ln2_b_row", [P, D])]
        ctx.callback(experts_sbuf.close)

        bank = [ctx.enter_context(nc.psum_tensor(f"bank{n}", [P, BANK], F32)) for n in range(8)]
        product_bank, scratch_bank, o_bank = bank[0:3], bank[3:5], bank[5:7]
        acc_bank = [bank[5], bank[6], bank[7], bank[0]]
        gu_bank, turn_bank, y_bank = bank[1], bank[2], bank[3:5]
        gather_bank = [bank[n] for n in (1, 2, 3, 4, 1, 2, 3, 4, 2)]

        ring_in = [sem(f"ring_in{n}") for n in range(RING)]
        chunk_used = sem("chunk_used")
        cond_in, cst_in, x_in, small_in = sem("cond_in"), sem("cst_in"), sem("x_in"), sem("small_in")
        b_ada_in = [sem("b_ada_in0"), sem("b_ada_in1")]
        mod_stored = [sem("mod_stored0"), sem("mod_stored1")]
        mod_in = [sem(f"mod_in{n}") for n in range(4)]
        b_gate_in = sem("b_gate_in")
        b_ada_t_in = sem("b_ada_t_in")
        cond_ready, cond_pad_ready = sem("cond_ready"), sem("cond_pad_ready")
        product_ready = sem("product_ready")
        bank_free = [sem(f"bank_free{n}") for n in range(N_ROT)]
        scratch_ready = sem("scratch_ready")
        scratch_free = [sem("scratch_free0"), sem("scratch_free1")]
        var_ready, std_ready = sem("var_ready"), sem("std_ready")
        norm_ready = sem("norm_ready")
        lb_diff_ready, lb_exp_ready = sem("lb_diff_ready"), sem("lb_exp_ready")
        forget_split, forget_log = sem("forget_split"), sem("forget_log")
        diff_ready, exp_ready = sem("diff_ready"), sem("exp_ready")
        q_ready, k_ready, key_sum_ready = sem("q_ready"), sem("k_ready"), sem("key_sum_ready")
        start_exp_ready, start_q_ready = sem("start_exp_ready"), sem("start_q_ready")
        end_diff_ready, end_exp_ready, end_key_ready = sem("end_diff_ready"), sem("end_exp_ready"), sem("end_key_ready")
        conv_ready = sem("conv_ready")
        gate_ready = sem("gate_ready")
        o_ready, square_ready, ms_ready, rms_ready = sem("o_ready"), sem("square_ready"), sem("ms_ready"), sem("rms_ready")
        a_ready = sem("a_ready")
        merged_ready = sem("merged_ready")
        ln1_in = sem("ln1_in")
        state_stored = sem("state_stored")
        silu_sh_ready = sem("silu_sh_ready")
        dve_step, act_step = sem("dve_step"), sem("act_step")

        def evacuated(product):
            n = PRODUCT_NO[product]
            return bank_free[n % N_ROT], n // N_ROT + 1

        def read_out(use):
            n = SCRATCH_NO[use]
            return scratch_free[n % 2], n // 2 + 1

        def rotating(product):
            if product == ("shared", 1):
                return bank[7]
            return product_bank[PRODUCT_NO[product] % N_ROT]

        def scratch(use):
            if use == ("logits",):
                return o_bank[0]
            return scratch_bank[SCRATCH_NO[use] % 2]

        mixer_done = sem("mixer_done")
        router_in, ln2_in = sem("router_in"), sem("ln2_in")
        h_lo_ready = sem("h_lo_ready")
        split_ready = sem("split_ready")
        chosen_ready, counted, listed = sem("chosen_ready"), sem("counted"), sem("listed")
        table_ready = sem("table_ready")
        piece_in = [sem(f"piece_in{n}") for n in range(RAW)]
        hi_ready, piece_used = sem("hi_ready"), sem("piece_used")
        low_up_ready, low_down_ready = sem("low_up_ready"), sem("low_down_ready")
        pick_ready, gathered = sem("pick_ready"), sem("gathered")
        x_act_ready, x_dve_ready = sem("x_act_ready"), sem("x_dve_ready")
        slot_gate_ready = sem("slot_gate_ready")
        gu_lo_ready, gu_sum_ready = sem("gu_lo_ready"), sem("gu_sum_ready")
        silu_ready, hid_ready = sem("silu_ready"), sem("hid_ready")
        turned, hid_hi_ready, hid_lo_ready, put_back_ready = sem("turned"), sem("hid_hi_ready"), sem("hid_lo_ready"), sem("put_back_ready")
        y0_ready, y_hi_ready, y_lo_ready, scattered = sem("y0_ready"), sem("y_hi_ready"), sem("y_lo_ready"), sem("scattered")
        split_free = sem("split_free")
        moe_done, out_ready, out_stored = sem("moe_done"), sem("out_ready"), sem("out_stored")

        def tile_out(j, k):
            s, tiles = (x_act_ready, ACT_TILES) if k in ACT_TILES else (x_dve_ready, DVE_TILES)
            return s, val(len(tiles) * j + tiles.index(k) + 1)

        def tok(g):
            return slice(g * P, (g + 1) * P)

        def rows8(w):
            return w.rearrange("(p k) n -> p k n", k=KD)

        def tiles(w):
            return w.rearrange("(k p) n -> p k n", p=P)

        def row(v):
            return v.partition_broadcast(P)

        def turns_after_first(eng):
            eng.wait_ge(table_ready, 2)
            return eng.value_load(last_turn[0:1, 0:1], min_val=1, max_val=MAX_ITEMS // ITEMS_PER_TURN - 1)

        block = ctx.enter_context(nc.Block())

        @block.sync
        def _(sp):
            def weights(n, chunk):
                kind, c = chunk
                slot = ring[:, n % RING, :]
                by_k = slot.rearrange("p (k n) -> p k n", k=KD)
                s = ring_in[n % RING]
                cols = slice(c * BANK, (c + 1) * BANK)
                if kind == "ada":
                    sp.dma_start(by_k, rows8(w_ada[0])[:, :, cols]).then_inc(s, 16)
                elif kind == "in":
                    sp.dma_start(by_k, tiles(w_in[0])[:, :, cols]).then_inc(s, 16)
                elif kind == "proj_hgrn":
                    sp.dma_start(slot.rearrange("p (k n) -> p k n", k=HEADS), tiles(w_proj_hgrn[0])).then_inc(s, 16)
                elif kind == "proj_fc":
                    half = slot.rearrange("p (b k n) -> p b k n", b=2, k=2)
                    sp.dma_start(half[:, 0], tiles(w_proj_fourier[0])).then_inc(s, 16)
                    sp.dma_start(half[:, 1], tiles(w_proj_conv[0])).then_inc(s, 16)
                elif kind == "out":
                    sp.dma_start(by_k, tiles(w_out[0])[:, :, cols]).then_inc(s, 16)
                elif kind == "shared_up":
                    half = slot.rearrange("p (b k n) -> p b k n", b=2, k=KD)
                    sp.dma_start(half[:, 0], rows8(w_sh_gate[0])).then_inc(s, 16)
                    sp.dma_start(half[:, 1], rows8(w_sh_up[0])).then_inc(s, 16)
                else:
                    sp.dma_start(slot[:, 0:2 * D].rearrange("p (k n) -> p k n", k=2), tiles(w_sh_down[0])).then_inc(s, 16)

            sp.dma_start(cond_t[:, 0, :], c_ctx.rearrange("(p k) -> p k", k=KD)).then_inc(cond_in, 16)
            sp.dma_start(cond_t[:, 1, :], c[0].rearrange("(p k) -> p k", k=KD)).then_inc(cond_in, 16)
            for n, chunk in enumerate(CHUNKS):
                if n >= RING:
                    sp.wait_ge(chunk_used, n - RING + 1)
                weights(n, chunk)
                if n == 0:
                    sp.dma_start(b_ada_t[:, :], b_ada[0, 0:2 * D].rearrange("(c p) -> p c", p=P), allow_slow_non_contiguous=True).then_inc(b_ada_t_in, 16)
                    sp.dma_start(resid[:, 0, :], x_prompt[0]).then_inc(x_in, 16)
                    sp.dma_start(resid[:, 1, :], x_sample[0]).then_inc(x_in, 16)
                    sp.dma_start(pos_sb, pos).then_inc(x_in, 16)
                    sp.dma_start(cst[:, :], table[:, 0:CST_KEEP]).then_inc(cst_in, 16)
                if n == len(ADA_EARLY) + 1:
                    sp.dma_start(dft[:, :], table[:, CST_KEEP:]).then_inc(small_in, 16)
                    sp.dma_start(mask_in, masks).then_inc(small_in, 16)
                    sp.dma_start(lb_in[:, :].rearrange("p (d h) -> p d h", d=2), hgrn_lb[0].rearrange("d (h p) -> p d h", p=P), allow_slow_non_contiguous=True).then_inc(small_in, 16)
                    sp.dma_start(norm_row[:, :], row(hgrn_norm[0])).then_inc(small_in, 16)
                    for ct in range(2):
                        sp.dma_start(conv_wt[:, ct, :], conv_w[0, :, ct * P:(ct + 1) * P].rearrange("k p -> p k"), allow_slow_non_contiguous=True).then_inc(small_in, 16)
                    sp.dma_start(state_in[:, :, :, :].rearrange("p d h v -> p (d h) v"),
                                  state_hgrn[0, 0].rearrange("d h k v -> k (d h) v")).then_inc(small_in, 16)

            def piece(kind, p, e):
                s = raw_slot(p)
                at = raw[:, s, :]
                if kind == "down":
                    src = w_exp_down[0, bass.ds(e, 1)].rearrange("a (p f) n -> p (a f) n", f=2)
                    for f in range(2):
                        sp.dma_start(at[:, f * D:(f + 1) * D], src[:, f]).then_inc(piece_in[s], 16)
                else:
                    ks = slice(kind * KD // 2, (kind + 1) * KD // 2)
                    for b, w in enumerate((w_exp_gate, w_exp_up)):
                        src = w[0, bass.ds(e, 1)].rearrange("a (p k) n -> p (a k) n", k=KD)
                        sp.dma_start(at[:, b * D:(b + 1) * D].rearrange("p (k n) -> p k n", n=DE),
                                     src[:, ks]).then_inc(piece_in[s], 16)

            def expert_of(n):
                return sp.value_load(item_expert[0:1, bass.ds(val(n), 1)], min_val=0, max_val=N_EXP - 1)

            def free(kind, n, p):
                if above_zero(p - RAW + 1):
                    if kind == "down":
                        sp.wait_ge(low_down_ready, val(n - 2))
                    else:
                        sp.wait_ge(low_up_ready, val(2 * (n - 2) + kind + 1))
                else:
                    sp.wait_ge(chunk_used, len(CHUNKS) - RING + 1 + p // 2)

            more_turns = turns_after_first(sp)

            def turn(j, first):
                e_before = None if first else expert_of(j * ITEMS_PER_TURN - 1)
                for q in range(ITEMS_PER_TURN):
                    e = expert_of(j * ITEMS_PER_TURN + q)
                    for kind, c in ((0, -1), (1, 0)):
                        c = 3 * q + c + (first and q == 0)
                        free(kind, j * ITEMS_PER_TURN + q, 12 * j + c)
                        piece(kind, (j, c), e)
                    if not (first and q == 0):
                        c = 3 * q + 1
                        free("down", j * ITEMS_PER_TURN + q, 12 * j + c)
                        piece("down", (j, c), e_before)
                    e_before = e
            turn(0, True)
            with sp.Fori(0, more_turns) as t:
                turn(Count(t, 1, 1), False)
            turns = Count(more_turns, 1, 1)
            e = expert_of(turns * ITEMS_PER_TURN - 1)
            free(0, turns * ITEMS_PER_TURN, 12 * turns - 1)
            piece("down", (turns, -1), e)

            for g, y in enumerate((y_prompt, y_sample)):
                sp.wait_ge(out_ready, g + 1)
                sp.dma_start(y[0], resid[:, g, :]).then_inc(out_stored, 16)
            sp.wait_ge(state_stored, 32)
            sp.wait_ge(out_stored, 32)

        @block.gpsimd
        def _(pool):
            def store_row(n):
                if n + 1 < len(ADA_ROWS):
                    if n >= 1:
                        pool.wait_ge(*evacuated(("ada", ADA_ROWS[n - 1])))
                    load_bias(n + 1)
                pool.wait_ge(*evacuated(("ada", ADA_ROWS[n])))
                nc.gpsimd.dma_start(mod_dram[:, n * BANK:(n + 1) * BANK], mod_row[:, n % 2, :]).then_inc(mod_stored[n % 2], 16)

            def load_bias(n):
                c = ADA_ROWS[n]
                nc.gpsimd.dma_start(b_ada_sb[:, n % 2, :], b_ada[:, c * BANK:(c + 1) * BANK].rearrange("a n -> (a n)").partition_broadcast(G)).then_inc(b_ada_in[n % 2], 16)

            def spread(v, dst):
                for s in mod_stored:
                    pool.wait_ge(s, 16 * (v + 1))
                for g in range(G):
                    nc.gpsimd.dma_start(dst[:, g, :], row(mod_dram[g, v * D:(v + 1) * D])).then_inc(mod_in[v], 16)

            load_bias(0)
            late = 0
            for what, at in schedule(True):
                if what == "stage":
                    continue
                if what == "step":
                    d, g, n = STEPS[at]
                    if d is not None:
                        pool.wait_ge(exp_ready, at + 1)
                        if at >= 2:
                            pool.wait_ge(scratch_ready, SCRATCH_NO[("step", at - 2)] + 1)
                        nc.gpsimd.tensor_tensor(lev_k[:, at % 2], kgate[:, d, :, tok(g)], lev_e[:, at % 2],
                                                ALU.mult).then_inc(k_ready, 1)
                elif at[0] == "ada":
                    store_row(late)
                    if late == 2:
                        spread(0, mod_a)
                    if late == 4:
                        spread(1, mod_b)
                    late += 1
                elif at[1] >= 7 and at[2] == 0:
                    if at[1] > 7:
                        pool.wait_ge(*evacuated(("in", at[1] - 1, 1)))
                    c = at[1] - 7
                    nc.gpsimd.dma_start(b_gate_sb[:, :], row(b_gate[0, c * BANK:(c + 1) * BANK])).then_inc(b_gate_in, 16)
            pool.wait_ge(merged_ready, 2 * G)
            spread(2, scale2)
            nc.gpsimd.drain().then_inc(mixer_done, 1)
            for n in range(late, len(ADA_ROWS)):
                store_row(n)
            spread(3, gate2)

            def low_down(j, c):
                p = 12 * j + c
                s = raw_slot((j, c))
                pool.wait_ge(piece_in[s], val(32 * (2 * j + c // RAW + 1)))
                pool.wait_ge(hi_ready, val(p + 1))
                if above_zero(p - N_SPLIT + 1):
                    pool.wait_ge(piece_used, val(p - N_SPLIT + 1))
                nc.gpsimd.tensor_tensor(w_lo[:, c % N_SPLIT, :], raw[:, s, :], w_hi[:, c % N_SPLIT, :].bitcast(F32),
                                        ALU.subtract).then_inc(low_down_ready, 1)

            def turn(j, first):
                for q in range(first, ITEMS_PER_TURN):
                    low_down(j, 3 * q + 1)

            pool.wait_ge(split_free, 1)
            more_turns = turns_after_first(pool)
            turn(0, True)
            with pool.Fori(0, more_turns) as t:
                turn(Count(t, 1, 1), False)
            low_down(Count(more_turns, 1, 1), -1)

        @block.scalar
        def _(act):
            own = [0]

            def step(ins):
                ins.then_inc(act_step, 1)
                own[0] += 1
                act.wait_ge(act_step, own[0])

            act.wait_ge(cond_in, 32)
            nc.scalar.activation(cond_s[:, :, :], cond_t[:, :, :].rearrange("p g k -> p k g"), ACT.Silu).then_inc(cond_ready, 1)

            def deviation(n):
                act.wait_ge(var_ready, n + 1)
                nc.scalar.activation(std[:, :], vareps[:, :], ACT.Sqrt).then_inc(std_ready, 1)

            def from_scratch(use, out, func=ACT.Copy):
                n = SCRATCH_NO[use]
                act.wait_ge(scratch_ready, n + 1)
                nc.scalar.activation(out, scratch(use)[:, 0:out.free_size()] if len(out.shape) == 2 else
                                     scratch(use)[:, 0:out.free_size()].rearrange("p (a b) -> p a b", a=out.shape[1]),
                                     func).then_inc(scratch_free[n % 2], 1)

            for c in ADA_EARLY:
                act.wait_ge(product_ready, PRODUCT_NO[("ada", c)] + 1)
                if c >= 2:
                    act.wait_ge(scratch_ready, SCRATCH_NO[("mod", c - 2)] + 1)
                nc.scalar.activation(mod_part[:, c % 2], rotating(("ada", c))[:, :], ACT.Copy).then_inc(evacuated(("ada", c))[0], 1)
                if c < 2:
                    deviation(c)
            for c in ADA_EARLY:
                act.wait_ge(*read_out(("mod", c)))
            for g in range(G):
                n = SCRATCH_NO[("h", g, 0)]
                act.wait_ge(scratch_ready, n + 1)
                for k in range(KD // 2):
                    ins = nc.scalar.activation(h_t[:, k, tok(g)], scratch(("h", g, 0))[:, k * P:(k + 1) * P], ACT.Identity,
                                               bias=mod_t[:, 0, k, g:g + 1], scale=mod_t[:, 1, k, g:g + 1])
                ins.then_inc(scratch_free[n % 2], 1)
            act.wait_ge(lb_diff_ready, 1)
            nc.scalar.activation(lb_e[:, :], lb_e[:, :], ACT.Exp).then_inc(lb_exp_ready, 1)

            def product_out(at):
                _, c, h = at
                n = PRODUCT_NO[at]
                act.wait_ge(product_ready, n + 1)
                b = rotating(at)
                pair = b[:, :].rearrange("p (a t) -> p a t", a=2)
                free = bank_free[n % N_ROT]
                if c in (2, 3):
                    nc.scalar.activation(fgate[:, c - 2, 2 * h:2 * h + 2, :], pair, ACT.Sigmoid)
                    nc.scalar.activation(kgate[:, c - 2, 2 * h:2 * h + 2, :], pair, ACT.Sigmoid, scale=-1.0).then_inc(free, 1)
                elif c == 0:
                    nc.scalar.activation(q_t[:, 2 * h:2 * h + 2, :], pair, ACT.Silu).then_inc(free, 1)
                elif c == 1:
                    nc.scalar.activation(value[:, h, :], b[:, :], ACT.Copy).then_inc(free, 1)
                elif c == 4:
                    nc.scalar.activation(out_gate[:, h, :], b[:, :], ACT.Silu).then_inc(free, 1)
                else:
                    out = {(5, 0): four, (5, 1): conv_b, (6, 0): conv_c, (6, 1): conv_h}[c, h]
                    nc.scalar.activation(out[:, :, :], pair, ACT.Copy).then_inc(free, 1)

            def forget_logs(d):
                act.wait_ge(forget_split, d + 1)
                both = decay[:, d, :, :].rearrange("p h t -> p (h t)")
                nc.scalar.activation(both, both, ACT.Ln)
                nc.scalar.activation(wide_tmp, wide_tmp, ACT.Ln, scale=1.0 / LN_SPLIT).then_inc(forget_log, 1)

            def gate_values(g):
                g_all = gates[:, g].rearrange("p b d -> p (b d)")
                nc.scalar.activation(g_all, g_all, ACT.Sigmoid).then_inc(gate_ready, 1)

            def stage(name):
                if name == "scan output":
                    n_scan = 2 * G * len(LEVELS)
                    act.wait_ge(q_ready, n_scan)
                    act.wait_ge(k_ready, n_scan)
                    for d in range(2):
                        nc.scalar.activation(lev_e[:, d], fgate[:, d, :, tok(1)], ACT.Exp).then_inc(start_exp_ready, 1)
                    for d in range(2):
                        act.wait_ge(end_diff_ready, d + 1)
                        nc.scalar.activation(lev_e[:, d], lev_e[:, d], ACT.Exp).then_inc(end_exp_ready, 1)
                elif name == "final keys":
                    for g in range(G):
                        from_scratch(("four1", g), four_f[:, g])
                    for g in range(G):
                        act.wait_ge(o_ready, g + 1)
                        if g:
                            act.wait_ge(ms_ready, g)
                        nc.scalar.activation(tmp[:, :, 0:P], o_bank[g][:, :].rearrange("p (h v) -> p h v", h=HEADS),
                                             ACT.Square).then_inc(square_ready, 1)
                        act.wait_ge(ms_ready, g + 1)
                        nc.scalar.activation(o_ss[:, :], o_ss[:, :], ACT.Sqrt).then_inc(rms_ready, 1)
                elif name == "final states":
                    for d in range(2):
                        act.wait_ge(end_key_ready, 2)
                        from_scratch(("ends", d), kd_t[:, d])
                elif name == "fourier":
                    for d in range(2):
                        from_scratch(("state", d), state_out[:, d])
                    for d in range(2):
                        act.wait_ge(*read_out(("state", d)))
                        act.dma_start(state_new[0, 0, d].rearrange("h k v -> k h v"), state_out[:, d]).then_inc(state_stored, 16)
                else:
                    act.wait_ge(conv_ready, 1)
                    from_scratch(("four2",), f_t[:, :, :])

            for what, at in schedule(True):
                if what == "stage":
                    stage(at)
                elif what == "step":
                    d, g, n = STEPS[at]
                    if d is not None:
                        act.wait_ge(diff_ready, at + 1)
                        nc.scalar.activation(lev_e[:, at % 2], lev_e[:, at % 2], ACT.Exp).then_inc(exp_ready, 1)
                elif at[0] == "in" and at[1] < 7:
                    if at == ("in", 4, 0):
                        forget_logs(1)
                    product_out(at)
                    if at == ("in", 0, 1):
                        forget_logs(0)

            for g in range(G):
                from_scratch(("a", g), a_t[:, :, tok(g)])
            act.wait_ge(*evacuated(("in", 12, 1)))
            gate_values(0)
            gate_values(1)
            for g in range(G):
                for a in range(2):
                    from_scratch(("merged", g, a), h_t[:, 4 * a:4 * a + 4, tok(g)])
            act.wait_ge(merged_ready, 2 * G)
            act.dma_start(ln1_rows[0], row(ln1_g[0])).then_inc(ln1_in, 16)
            act.dma_start(ln1_rows[1], row(ln1_b[0])).then_inc(ln1_in, 16)
            act.wait_ge(state_stored, 32)
            act.drain().then_inc(mixer_done, 1)

            for n in (2, 3):
                deviation(n)
            act.wait_ge(mixer_done, 4)
            act.dma_start(w_rt[:, :, :], rows8(w_router[0])).then_inc(router_in, 16)
            act.dma_start(b_rt[:, :], row(b_router[0])).then_inc(router_in, 16)
            act.dma_start(ln2_rows[0][:, :], row(ln2_g[0])).then_inc(ln2_in, 16)
            act.dma_start(ln2_rows[1][:, :], row(ln2_b[0])).then_inc(ln2_in, 16)
            for g in range(G):
                if g:
                    for n in (4, 5):
                        deviation(n)
                act.wait_ge(norm_ready, G + g + 1)
                nc.scalar.activation(h_hi[:, g], h2_tok[:, g, :].rearrange("p (q k) -> p k q", k=KD),
                                     ACT.Copy).then_inc(split_ready, 1)
                for a in range(2):
                    from_scratch(("h2", g, a), h_t[:, 4 * a:4 * a + 4, tok(g)])
            from_scratch(("logits",), score[:, :, :], ACT.Sigmoid)

            def silu_shared(f):
                act.wait_ge(product_ready, PRODUCT_NO[("shared", f)] + 1)
                if f:
                    act.wait_ge(*evacuated(("shared", f - 1)))
                nc.scalar.activation(silu_sh[:, :], rotating(("shared", f))[:, 0:TOK], ACT.Silu).then_inc(silu_sh_ready, 1)

            act.wait_ge(scratch_ready, SCRATCH_NO[("rows",)] + 1)
            nc.scalar.activation(rows_t[:, :, :, :].rearrange("p a g t -> p (a g t)"),
                                 scratch(("rows",))[0:N_EXP, :], ACT.Copy).then_inc(scratch_free[SCRATCH_NO[("rows",)] % 2], 1)
            for f in range(2):
                silu_shared(f)

            def high(j, c, kind):
                p = 12 * j + c
                s = raw_slot((j, c))
                act.wait_ge(piece_in[s], val(32 * (2 * j + c // RAW + 1)))
                if above_zero(p - N_SPLIT + 1):
                    act.wait_ge(piece_used, val(p - N_SPLIT + 1))
                out, src = w_hi[:, c % N_SPLIT, :], raw[:, s, :]
                if kind == "up":
                    out = out.rearrange("p (k b n) -> p k b n", k=KD // 2, b=2)
                    src = src.rearrange("p (b k n) -> p k b n", k=KD // 2, b=2)
                nc.scalar.activation(out, src, ACT.Copy).then_inc(hi_ready, 1)

            def need(s, value):
                if above_zero(value):
                    act.wait_ge(s, val(value))

            def turned_out(n):
                act.wait_ge(turned, val(n + 1))
                nc.scalar.activation(hid_t[:, :, 0:SLOTS], turn_bank[:, 0:2 * SLOTS].rearrange("p (f s) -> p f s", f=2),
                                     ACT.Copy).then_inc(hid_hi_ready, 1)

            def y_high(m, h, last=False):
                if h == 0:
                    act.wait_ge(y0_ready, val(m + 1))
                else:
                    act.wait_ge(piece_used, val(3 * m + (3 if last else 5)))
                need(scattered, m)
                nc.scalar.activation(y_hi[:, h, :], y_bank[h][:, :], ACT.Copy).then_inc(y_hi_ready, 1)

            def gu_low(m):
                act.wait_ge(piece_used, val(3 * m + 1 if above_zero(m) else 2))
                need(gu_sum_ready, m)
                nc.scalar.activation(gu_lo[:, :], gu_bank[SLOTS:2 * SLOTS, :], ACT.Copy).then_inc(gu_lo_ready, 1)

            def silu(m):
                act.wait_ge(gu_sum_ready, val(m + 1))
                nc.scalar.activation(silu_g[:, :], gu[:, 0:DE], ACT.Silu).then_inc(silu_ready, 1)

            def gather_out(j):
                act.wait_ge(gathered, val((KD + 1) * j + 1))
                need(hid_ready, j * ITEMS_PER_TURN)
                nc.scalar.activation(slot_gate[:, :], gather_bank[0][0:SLOTS, 0:ITEMS_PER_TURN], ACT.Copy).then_inc(slot_gate_ready, 1)
                for k in ACT_TILES:
                    act.wait_ge(gathered, val((KD + 1) * j + k + 2))
                    nc.scalar.activation(x_g[:, k], gather_bank[k + 1][:, :].rearrange("p (q s) -> p q s", q=ITEMS_PER_TURN),
                                         ACT.Copy).then_inc(x_act_ready, 1)

            def turn(j, first):
                for q in range(ITEMS_PER_TURN):
                    n = j * ITEMS_PER_TURN + q
                    start = first and q == 0
                    high(j, 3 * q - 1 + start, "up")
                    high(j, 3 * q + start, "up")
                    if not start:
                        gu_low(n - 1)
                        if not (first and q == 1):
                            turned_out(n - 1)
                        high(j, 3 * q + 1, "down")
                        silu(n - 1)
                        if not (first and q == 1):
                            for h in range(2):
                                y_high(n - 2, h)
                    if q == 0:
                        gather_out(j)

            act.wait_ge(split_free, 1)
            more_turns = turns_after_first(act)
            turn(0, True)
            with act.Fori(0, more_turns) as t:
                turn(Count(t, 1, 1), False)
            turns = Count(more_turns, 1, 1)
            n_items = turns * ITEMS_PER_TURN
            gu_low(n_items - 1)
            turned_out(n_items - 1)
            high(turns, -1, "down")
            silu(n_items - 1)
            for h in range(2):
                y_high(n_items - 2, h)
            turned_out(n_items)
            for h in range(2):
                y_high(n_items - 1, h, True)
            for n in range(6, 8):
                deviation(n)

        @block.vector
        def _(dve):
            own = [0]

            def step(ins):
                ins.then_inc(dve_step, 1)
                own[0] += 1
                dve.wait_ge(dve_step, own[0])

            def need(s, value):
                if above_zero(value):
                    dve.wait_ge(s, val(value))

            norms = [0]

            def statistics(x):
                for h in range(2):
                    ins = nc.vector.bn_stats(bn[:, h, :], x[:, h * BANK:(h + 1) * BANK])
                step(ins)
                step(nc.vector.bn_aggr(mv[:, :], bn[:, :, :]))
                nc.vector.tensor_scalar(vareps[:, :], mv[:, 1:2], LN_EPS, None, ALU.add).then_inc(var_ready, 1)

            def inverse_root():
                norms[0] += 1
                dve.wait_ge(std_ready, norms[0])
                step(nc.vector.reciprocal(rstd[:, :], std[:, :]))

            def normalize(out, x, gain=None, bias=None):
                statistics(x)
                if gain is None:
                    inverse_root()
                    return nc.vector.tensor_scalar(out, x, mv[:, 0:1], rstd[:, 0:1], ALU.subtract, ALU.mult)
                step(nc.vector.scalar_tensor_tensor(out, x, mv[:, 0:1], gain, ALU.subtract, ALU.mult))
                inverse_root()
                return nc.vector.scalar_tensor_tensor(out, out, rstd[:, 0:1], bias, ALU.mult, ALU.add)

            dve.wait_ge(cond_ready, 1)
            step(nc.vector.memset(cond_pad, 0.0))
            nc.vector.tensor_copy(cond_pad[:, :, 0:G], cond_s[:, :, :]).then_inc(cond_pad_ready, 1)

            dve.wait_ge(x_in, 48)
            step(nc.vector.tensor_tensor(resid[:, 1, :], resid[:, 1, :], pos_sb, ALU.add))
            for g in range(G):
                normalize(h_tok[:, g, :], resid[:, g, :]).then_inc(norm_ready, 1)
                dve.wait_ge(norm_ready, g + 1)
            for e in (0, P + 1):
                nc.vector.memset(conv_z[:, :, :, e:e + 1], 0.0)
            dve.wait_ge(b_ada_t_in, 16)
            for n, c in enumerate(ADA_EARLY):
                which, half = c // 2, c % 2
                use = SCRATCH_NO[("mod", c)]
                dve.wait_ge(scratch_ready, use + 1)
                nc.vector.scalar_tensor_tensor(
                    mod_t[:, which, half * KD // 2:(half + 1) * KD // 2, :], scratch(("mod", c))[:, 0:KD // 2 * G].rearrange("p (k g) -> p k g", g=G),
                    float(which), b_ada_t[:, c * KD // 2:(c + 1) * KD // 2].unsqueeze(2).broadcast_to([P, KD // 2, G]),
                    ALU.add, ALU.add).then_inc(scratch_free[use % 2], 1)
            for c in ADA_EARLY:
                dve.wait_ge(*read_out(("mod", c)))
            for g in range(G):
                n = SCRATCH_NO[("h", g, 1)]
                dve.wait_ge(scratch_ready, n + 1)
                for k in range(KD // 2, KD):
                    ins = nc.vector.tensor_scalar(h_t[:, k, tok(g)], scratch(("h", g, 1))[:, (k - KD // 2) * P:(k - KD // 2 + 1) * P],
                                                  mod_t[:, 1, k, g:g + 1], mod_t[:, 0, k, g:g + 1], ALU.mult, ALU.add)
                ins.then_inc(scratch_free[n % 2], 1)

            def modulation_row(n):
                c = ADA_ROWS[n]
                dve.wait_ge(product_ready, PRODUCT_NO[("ada", c)] + 1)
                dve.wait_ge(b_ada_in[n % 2], 16 * (n // 2 + 1))
                if n >= 2:
                    dve.wait_ge(mod_stored[n % 2], 16 * (n // 2))
                bank_in, mod = rotating(("ada", c)), mod_row[:, n % 2, :]
                one = 1.0 if n // 2 == 2 else 0.0
                step(nc.vector.scalar_tensor_tensor(mod, bank_in[0:G, :], one, b_ada_sb[:, n % 2, :], ALU.add, ALU.add))
                for i in range(1, COL_GROUPS):
                    ins = nc.vector.tensor_tensor(mod, bank_in[i * COLS:i * COLS + G, :], mod, ALU.add)
                    if i < COL_GROUPS - 1:
                        step(ins)
                ins.then_inc(evacuated(("ada", c))[0], 1)

            dve.wait_ge(small_in, 7 * 16)
            nc.vector.tensor_copy(mask_sb[:, :, :].rearrange("p m t -> p (m t)"), mask_in)
            nc.vector.tensor_tensor(lb_e[:, :], lb_in[:, :], lb_in[:, :], ALU.subtract).then_inc(lb_diff_ready, 1)
            dve.wait_ge(lb_exp_ready, 1)
            step(nc.vector.reciprocal(lb[:, :], lb_e[:, :]))
            step(nc.vector.tensor_tensor(lb_one[:, :], lb_e[:, :], lb[:, :], ALU.mult))
            step(nc.vector.tensor_tensor(lb[:, :], lb_one[:, :], lb_one[:, :], ALU.subtract))
            step(nc.vector.tensor_scalar(lb_one[:, :], lb[:, :], -1.0, 1.0, ALU.mult, ALU.add))

            def forget(d):
                for h in range(2):
                    dve.wait_ge(*evacuated(("in", 2 + d, h)))
                for h in range(HEADS):
                    b = d * HEADS + h
                    nc.vector.tensor_scalar(fgate[:, d, h, :], fgate[:, d, h, :], lb_one[:, b:b + 1], lb[:, b:b + 1], ALU.mult, ALU.add)
                    ins = nc.vector.tensor_scalar(kgate[:, d, h, :], kgate[:, d, h, :], lb_one[:, b:b + 1], None, ALU.mult)
                step(ins)
                f_all = fgate[:, d, :, :].rearrange("p h t -> p (h t)")
                log_all = decay[:, d, :, :].rearrange("p h t -> p (h t)")
                nc.vector.tensor_scalar(log_all, f_all, LN_SPLIT, None, ALU.max)
                nc.vector.tensor_scalar(wide_tmp, f_all, F_MIN, LN_SPLIT, ALU.max, ALU.min).then_inc(forget_split, 1)
                dve.wait_ge(forget_log, d + 1)
                step(nc.vector.tensor_tensor(log_all, log_all, wide_tmp, ALU.add))
                for h in range(HEADS):
                    for g in range(G):
                        ins = nc.vector.tensor_tensor_scan(fgate[:, d, h, tok(g)], ones, decay[:, d, h, tok(g)], 0.0, ALU.mult, ALU.add)
                step(ins)
                if d == 1:
                    step(nc.vector.tensor_copy(scan_end[:, :, :], fgate[:, 1].rearrange("p h (g t) -> p h g t", g=G)[:, :, :, P - 1]))
                    step(nc.vector.tensor_tensor(f_all, log_all, f_all, ALU.subtract))
                    for h in range(HEADS):
                        for g in range(G):
                            ins = nc.vector.tensor_scalar(fgate[:, 1, h, tok(g)], fgate[:, 1, h, tok(g)], scan_end[:, h, g:g + 1], None, ALU.add)
                    step(ins)

            forget(0)

            def level_diffs(s):
                d, g, n = STEPS[s]
                half = LEVELS[n]
                b = fgate[:, d, :, tok(g)].rearrange("p h (m a i) -> p h m a i", a=2, i=half)
                e = lev_e[:, s % 2].rearrange("p h (m a i) -> p h m a i", a=2, i=half)
                at = b[:, :, :, 0, half - 1:half] if d == 0 else b[:, :, :, 1, 0:1]
                mid = at.broadcast_to([P, HEADS, P // (2 * half), half])
                below, above = (0, 1) if d == 0 else (1, 0)
                if s >= 2:
                    dve.wait_ge(k_ready, s - 1)
                nc.vector.tensor_tensor(e[:, :, :, below, :], mid, b[:, :, :, below, :], ALU.subtract)
                nc.vector.tensor_tensor(e[:, :, :, above, :], b[:, :, :, above, :], mid, ALU.subtract).then_inc(diff_ready, 1)

            def take_scores(s):
                d, g, n = STEPS[s]
                m = N_MASK - 1 if d is None else d * len(LEVELS) + n
                use = SCRATCH_NO[("step", s)]
                dve.wait_ge(scratch_ready, use + 1)
                if s:
                    dve.wait_ge(*read_out(("step", s - 1)))
                nc.vector.copy_predicated(scores[:, g], mask_sb[:, m:m + 1, :].broadcast_to([P, HEADS, P]),
                                          scratch(("step", s))[:, :].rearrange("p (h t) -> p h t", h=HEADS)).then_inc(scratch_free[use % 2], 1)

            def scan_step(s):
                d, g, n = STEPS[s]
                if d is not None:
                    level_diffs(s)
                if s >= 2:
                    take_scores(s - 2)
                if d is None:
                    nc.vector.tensor_tensor(lev_k[:, s % 2], kgate[:, 0, :, tok(g)], kgate[:, 1, :, tok(g)], ALU.add).then_inc(key_sum_ready, 1)
                else:
                    dve.wait_ge(exp_ready, s + 1)
                    nc.vector.tensor_tensor(lev_q[:, s % 2], q_t[:, :, tok(g)], lev_e[:, s % 2], ALU.mult).then_inc(q_ready, 1)

            def convolution():
                for p in [("in", 5, 1), ("in", 6, 0), ("in", 6, 1)]:
                    dve.wait_ge(*evacuated(p))
                by_g = lambda t, ct: t[:, ct, :].rearrange("p (g t) -> p g t", g=G)
                for ct in range(2):
                    ins = nc.vector.tensor_tensor(conv_z[:, ct, :, 1:P + 1], by_g(conv_c, ct), by_g(conv_h, ct), ALU.mult)
                step(ins)
                for tap in (1, 0, 2):
                    for ct in range(2):
                        z, y, w = conv_z[:, ct, :, tap:tap + P], by_g(c_t, ct), conv_wt[:, ct, tap:tap + 1]
                        if tap == 1:
                            ins = nc.vector.tensor_scalar(y, z, w, None, ALU.mult)
                        else:
                            ins = nc.vector.scalar_tensor_tensor(y, z, w, y, ALU.mult, ALU.add)
                    step(ins)
                nc.vector.tensor_tensor(c_t[:, :, :], c_t[:, :, :], conv_b[:, :, :], ALU.mult).then_inc(conv_ready, 1)

            def stage(name):
                if name == "scan output":
                    for s in range(len(STEPS) - 2, len(STEPS)):
                        take_scores(s)
                    for d in range(2):
                        dve.wait_ge(start_exp_ready, d + 1)
                        nc.vector.tensor_tensor(lev_q[:, d], q_t[:, :, tok(1)], lev_e[:, d], ALU.mult).then_inc(start_q_ready, 1)
                    dve.wait_ge(start_q_ready, 2)
                    for d in range(2):
                        end = P - 1 if d == 0 else 0
                        b = fgate[:, d, :, tok(0)]
                        nc.vector.tensor_tensor(lev_e[:, d], b[:, :, end:end + 1].broadcast_to([P, HEADS, P]), b, ALU.subtract).then_inc(end_diff_ready, 1)
                    for d in range(2):
                        dve.wait_ge(end_exp_ready, d + 1)
                        nc.vector.tensor_tensor(kd_sb[:, d], kgate[:, d, :, tok(0)], lev_e[:, d], ALU.mult).then_inc(end_key_ready, 1)
                    for g in range(G):
                        step(nc.vector.tensor_tensor(out_gate[:, g, :], out_gate[:, g, :], norm_row[:, :], ALU.mult))
                elif name == "final keys":
                    for g in range(G):
                        dve.wait_ge(square_ready, g + 1)
                        step(nc.vector.reduce_sum(o_ss[:, :], tmp[:, :, 0:P], axis=AXX))
                        nc.vector.tensor_scalar(o_ss[:, :], o_ss[:, :], 1.0 / DK, RMS_EPS, ALU.mult, ALU.add).then_inc(ms_ready, 1)
                        dve.wait_ge(rms_ready, g + 1)
                        step(nc.vector.reciprocal(o_r[:, :], o_ss[:, :]))
                        gate = out_gate[:, g, :].rearrange("p (h v) -> p h v", h=HEADS)
                        step(nc.vector.tensor_tensor(gate, gate, o_r[:, :].unsqueeze(2).broadcast_to([P, HEADS, DK]), ALU.mult))
                        nc.vector.tensor_tensor(out_gate[:, g, :], o_bank[g][:, :], out_gate[:, g, :], ALU.mult).then_inc(a_ready, 1)

            late = 0
            for what, at in schedule(True):
                if what == "stage":
                    stage(at)
                elif what == "step":
                    if at == 0:
                        for h in range(2):
                            dve.wait_ge(*evacuated(("in", 0, h)))
                    scan_step(at)
                elif at == ("in", 4, 0):
                    forget(1)
                elif at[0] == "ada":
                    modulation_row(late)
                    late += 1
                elif at[1] >= 7:
                    if at == ("in", 7, 0):
                        convolution()
                    _, c, g = at
                    b, h = (c - 7) // 2, (c - 7) % 2
                    dve.wait_ge(product_ready, PRODUCT_NO[at] + 1)
                    dve.wait_ge(b_gate_in, 16 * (c - 6))
                    nc.vector.tensor_tensor(gates[:, g, b, h * BANK:(h + 1) * BANK], rotating(at)[:, :], b_gate_sb[:, :],
                                            ALU.add).then_inc(evacuated(at)[0], 1)
            for g in range(G):
                dve.wait_ge(gate_ready, g + 1)
                for h in range(2):
                    cols = slice(h * BANK, (h + 1) * BANK)
                    for i, b in enumerate(BRANCH_ORDER):
                        at = ("proj", g, h, b)
                        s, full = evacuated(at)
                        dve.wait_ge(product_ready, PRODUCT_NO[at] + 1)
                        out = merged[:, g, cols] if i == 0 else wide_tmp[:, 0:BANK]
                        nc.vector.tensor_tensor(out, rotating(at)[:, :], gates[:, g, b, cols], ALU.mult).then_inc(s, 1)
                        dve.wait_ge(s, full)
                        if i:
                            ins = nc.vector.tensor_tensor(merged[:, g, cols], merged[:, g, cols], wide_tmp[:, 0:BANK], ALU.add)
                            if i < NB - 1:
                                step(ins)
                    ins.then_inc(merged_ready, 1)
                    dve.wait_ge(merged_ready, 2 * g + h + 1)

            dve.wait_ge(mod_in[0], 32)

            def residual(h, g):
                cols = slice(h * BANK, (h + 1) * BANK)
                at = ("out", h, g)
                s, full = evacuated(at)
                dve.wait_ge(product_ready, PRODUCT_NO[at] + 1)
                nc.vector.tensor_tensor(mod_a[:, g, cols], rotating(at)[:, :], mod_a[:, g, cols], ALU.mult).then_inc(s, 1)
                dve.wait_ge(s, full)
                step(nc.vector.scalar_tensor_tensor(resid[:, g, cols], resid[:, g, cols], ALPHA, mod_a[:, g, cols], ALU.mult, ALU.add))

            def two_norms(g):
                step(normalize(resid[:, g, :], resid[:, g, :], ln1_rows[0], ln1_rows[1]))
                normalize(h2_tok[:, g, :], resid[:, g, :], scale2[:, g, :], mod_b[:, g, :]).then_inc(norm_ready, 1)
                dve.wait_ge(norm_ready, G + g + 1)

            for h in range(2):
                residual(h, 0)
                if h == 0:
                    residual(h, 1)
            dve.wait_ge(ln1_in, 32)
            dve.wait_ge(mod_in[1], 32)
            dve.wait_ge(mod_in[2], 32)
            two_norms(0)
            residual(1, 1)
            nc.vector.drain().then_inc(mixer_done, 1)
            two_norms(1)
            for n in range(late, len(ADA_ROWS)):
                modulation_row(n)
            dve.wait_ge(norm_ready, 2 * G)
            dve.wait_ge(mixer_done, 4)
            for g in range(G):
                dve.wait_ge(split_ready, g + 1)
                nc.vector.tensor_tensor(h_lo[:, g], h2_tok[:, g, :].rearrange("p (q k) -> p k q", k=KD), h_hi[:, g].bitcast(F32), ALU.subtract).then_inc(h_lo_ready, 1)

            def hidden_shared(f):
                at = ("shared", f)
                dve.wait_ge(silu_sh_ready, f + 1)
                nc.vector.tensor_tensor(hid_sh[:, f, :], silu_sh[:, :], rotating(at)[:, TOK:2 * TOK], ALU.mult).then_inc(evacuated(at)[0], 1)

            dve.wait_ge(router_in, 32)
            dve.wait_ge(*read_out(("logits",)))
            step(nc.vector.tensor_tensor(biased[:, :, :], score[:, :, :], b_rt[:, :].unsqueeze(1).broadcast_to([P, G, N_EXP]), ALU.add))
            for g in range(G):
                step(nc.vector.max(top8[:, g, :], biased[:, g, :]))
                step(nc.vector.match_replace(left_over[:, g, :], top8[:, g, :], biased[:, g, :], -1e30))
            nc.vector.tensor_tensor(chosen[:, :, :], left_over[:, :, :], biased[:, :, :], ALU.not_equal).then_inc(chosen_ready, 1)
            dve.wait_ge(chosen_ready, 1)
            step(nc.vector.tensor_tensor(weight[:, :, :], score[:, :, :], chosen[:, :, :], ALU.mult))
            step(nc.vector.reduce_sum(total_w[:, :], weight[:, :, :], axis=AXX))
            step(nc.vector.tensor_scalar(total_w[:, :], total_w[:, :], 1e-20, None, ALU.add))
            step(nc.vector.reciprocal(total_w[:, :], total_w[:, :]))
            for g in range(G):
                step(nc.vector.tensor_scalar(weight[:, g, :], weight[:, g, :], total_w[:, g:g + 1], ROUTED_SCALE, ALU.mult, ALU.mult))

            def taken(use, ins):
                s, full = read_out(use)
                ins.then_inc(s, 1)
                dve.wait_ge(s, full)

            def awaited(use):
                dve.wait_ge(scratch_ready, SCRATCH_NO[use] + 1)
                return scratch(use)

            b = awaited(("place",))
            taken(("place",), nc.vector.scalar_tensor_tensor(
                place[:, :, :], b[:, 0:G * N_EXP].rearrange("p (g e) -> p g e", g=G), 1.0, chosen[:, :, :], ALU.add, ALU.mult))
            b = awaited(("count",))
            taken(("count",), nc.vector.tensor_copy(counts[0:N_EXP, :], b[0:N_EXP, 0:1]))
            step(nc.vector.tensor_scalar(has_chunk[0:N_EXP, :], con("chunk_at")[0:N_EXP, :], counts[0:N_EXP, :], None, ALU.is_lt))
            nc.vector.reduce_sum(n_chunks[0:N_EXP, :], has_chunk[0:N_EXP, :], axis=AXX).then_inc(counted, 1)
            b = awaited(("before",))
            step(nc.vector.tensor_scalar(first_item[:, :], con("chunk_no")[0:N_EXP, :], b[0:N_EXP, 0:1], None, ALU.add))
            taken(("before",), nc.vector.tensor_scalar(last_turn[0:1, 1:2], b[0:1, 1:2], -1.0, None, ALU.add))
            nc.vector.tensor_scalar(last_turn[0:1, 0:1], last_turn[0:1, 1:2], 2, None, ALU.logical_shift_right).then_inc(table_ready, 1)
            nc.vector.memset(of_item[:, :], 0.0)
            step(nc.vector.memset(at_item[:, :], 0.0))
            for ch in range(MAX_CHUNKS):
                step(nc.vector.tensor_scalar(is_item[:, :], con("item_no")[0:N_EXP, :], first_item[:, ch:ch + 1], has_chunk[0:N_EXP, ch:ch + 1], ALU.is_equal, ALU.mult))
                nc.vector.tensor_tensor(of_item[:, :], of_item[:, :], is_item[:, :], ALU.add)
                nc.vector.scalar_tensor_tensor(at_item[:, :], is_item[:, :], float(ch * SLOTS), at_item[:, :], ALU.mult, ALU.add).then_inc(listed, 1)
                dve.wait_ge(listed, ch + 1)
            b = awaited(("items",))
            nc.vector.tensor_copy(item_expert[0:1, :], b[0:1, 0:MAX_ITEMS]).then_inc(table_ready, 1)
            taken(("items",), nc.vector.tensor_copy(item_at[:, :], b[:, P:P + MAX_ITEMS]))
            b = awaited(("item_rows",))
            two = b[:, 0:2 * G * MAX_ITEMS].rearrange("p (a g i) -> p a g i", a=2, g=G)
            nc.vector.tensor_tensor(item_place[:, :, :], two[:, 0], item_at[:, :].unsqueeze(1).broadcast_to([P, G, MAX_ITEMS]), ALU.subtract)
            taken(("item_rows",), nc.vector.tensor_copy(item_weight[:, :, :], two[:, 1]))
            for f in range(2):
                hidden_shared(f)

            def low(j, c):
                p = 12 * j + c
                s = raw_slot((j, c))
                dve.wait_ge(piece_in[s], val(32 * (2 * j + c // RAW + 1)))
                dve.wait_ge(hi_ready, val(p + 1))
                if above_zero(p - N_SPLIT + 1):
                    dve.wait_ge(piece_used, val(p - N_SPLIT + 1))
                out, hi = (w[:, c % N_SPLIT, :].rearrange("p (k b n) -> p k b n", k=KD // 2, b=2) for w in (w_lo, w_hi))
                src = raw[:, s, :].rearrange("p (b k n) -> p k b n", k=KD // 2, b=2)
                nc.vector.tensor_tensor(out, src, hi.bitcast(F32), ALU.subtract).then_inc(low_up_ready, 1)

            def turned_out(n, q, first):
                if first:
                    dve.wait_ge(turned, val(n + 1))
                else:
                    dve.wait_ge(hid_hi_ready, val(n))
                    nc.vector.tensor_tensor(hid_t[:, :, SLOTS:2 * SLOTS], turn_bank[:, 0:2 * SLOTS].rearrange("p (f s) -> p f s", f=2),
                                            hid_t[:, :, 0:SLOTS].bitcast(F32), ALU.subtract).then_inc(hid_lo_ready, 1)
                if q is not None:
                    need(scattered, n - 2)
                    nc.vector.tensor_copy(put_back[:, q], turn_bank[:, P:P + G * P].rearrange("p (g t) -> p g t", g=G)).then_inc(put_back_ready, 1)

            def y_low(m, h):
                dve.wait_ge(y_hi_ready, val(2 * m + h + 1))
                nc.vector.tensor_tensor(y_lo[:, h, :], y_bank[h][:, :], y_hi[:, h, :].bitcast(F32), ALU.subtract).then_inc(y_lo_ready, 1)

            def gu_sum(m):
                dve.wait_ge(gu_lo_ready, val(m + 1))
                need(silu_ready, m)
                need(hid_ready, m)
                nc.vector.tensor_tensor(gu[:, :], gu_bank[0:SLOTS, :], gu_lo[:, :], ALU.add).then_inc(gu_sum_ready, 1)

            def hidden(m, q):
                dve.wait_ge(silu_ready, val(m + 1))
                need(turned, m + 1)
                nc.vector.scalar_tensor_tensor(hid[:, :], silu_g[:, :], slot_gate[:, q:q + 1], gu[:, DE:2 * DE], ALU.mult, ALU.mult).then_inc(hid_ready, 1)

            def gather_out(j):
                for k in DVE_TILES:
                    dve.wait_ge(gathered, val((KD + 1) * j + k + 2))
                    nc.vector.tensor_copy(x_g[:, k], gather_bank[k + 1][:, :].rearrange("p (q s) -> p q s", q=ITEMS_PER_TURN)).then_inc(x_dve_ready, 1)

            def picks(j):
                need(turned, j * ITEMS_PER_TURN)
                need(gathered, (KD + 1) * j)
                items = bass.ds(val(j * ITEMS_PER_TURN), ITEMS_PER_TURN)
                for g in range(G):
                    nc.vector.tensor_tensor(
                        pick[:, g], con("slot_no").unsqueeze(1).broadcast_to([P, ITEMS_PER_TURN, 2 * SLOTS]),
                        item_place[:, g, items].unsqueeze(2).broadcast_to([P, ITEMS_PER_TURN, 2 * SLOTS]),
                        ALU.is_equal)
                nc.vector.tensor_copy(gate4[:, :, :], item_weight[:, :, items]).then_inc(pick_ready, 1)

            def turn(j, first):
                for q in range(ITEMS_PER_TURN):
                    n = j * ITEMS_PER_TURN + q
                    start = first and q == 0
                    low(j, 3 * q - 1 + start)
                    if not start:
                        gu_sum(n - 1)
                        turned_out(n - 1, (q - 1) % ITEMS_PER_TURN, first and q == 1)
                    if q:
                        low(j, 3 * q + start)
                    else:
                        picks(j)
                    if not start:
                        hidden(n - 1, (q - 1) % ITEMS_PER_TURN)
                    if not (first and q < 2):
                        for h in range(2):
                            y_low(n - 2, h)
                    if q == 0:
                        gather_out(j)
                        low(j, 3 * q + start)

            more_turns = turns_after_first(dve)
            turn(0, True)
            with dve.Fori(0, more_turns) as t:
                turn(Count(t, 1, 1), False)
            turns = Count(more_turns, 1, 1)
            n_items = turns * ITEMS_PER_TURN
            gu_sum(n_items - 1)
            turned_out(n_items - 1, ITEMS_PER_TURN - 1, False)
            hidden(n_items - 1, ITEMS_PER_TURN - 1)
            for h in range(2):
                y_low(n_items - 2, h)
            turned_out(n_items, None, False)
            for h in range(2):
                y_low(n_items - 1, h)

            dve.wait_ge(moe_done, 1)
            dve.wait_ge(ln2_in, 32)
            dve.wait_ge(mod_in[3], 32)
            for g in range(G):
                for h in range(2):
                    cols = slice(h * BANK, (h + 1) * BANK)
                    step(nc.vector.tensor_tensor(gate2[:, g, cols], acc_bank[2 * g + h][:, :], gate2[:, g, cols], ALU.mult))
                step(nc.vector.scalar_tensor_tensor(resid[:, g, :], resid[:, g, :], ALPHA, gate2[:, g, :], ALU.mult, ALU.add))
                normalize(resid[:, g, :], resid[:, g, :], ln2_rows[0][:, :], ln2_rows[1][:, :]).then_inc(out_ready, 1)

        @block.tensor
        def _(pe):
            mm = nc.tensor.matmul

            def need(s, value):
                if above_zero(value):
                    pe.wait_ge(s, val(value))

            def bank_for(product):
                n = PRODUCT_NO[product]
                if n >= N_ROT:
                    pe.wait_ge(bank_free[n % N_ROT], n // N_ROT)
                return rotating(product)

            def scratch_for(use):
                n = SCRATCH_NO[use]
                if n >= 2:
                    pe.wait_ge(scratch_free[n % 2], n // 2)
                return scratch(use)

            def arrived(chunk):
                slot, full = chunk_arrived(chunk)
                pe.wait_ge(ring_in[slot], full)
                return ring[:, slot, :]

            def modulation(c, cond=cond_s, rows=G):
                out = bank_for(("ada", c))
                w = arrived(("ada", c)).rearrange("p (k n) -> p k n", k=KD)
                for k in range(KD):
                    i = k % COL_GROUPS
                    ins = mm(out[i * COLS:i * COLS + rows, :], cond[:, k, :], w[:, k, :], start=k < COL_GROUPS,
                             stop=k >= KD - COL_GROUPS, tile_position=(0, i * COLS))
                ins.then_inc(product_ready, 1)
                nc.tensor.drain().then_inc(chunk_used, 1)

            def turn_tiles(use, tiles_in):
                out = scratch_for(use)
                for i, t in enumerate(tiles_in):
                    ins = nc.tensor.transpose(out[0:t.free_size(), i * P:i * P + t.partition_size()], t, ident)
                ins.then_inc(scratch_ready, 1)

            def w_in_product(at):
                _, c, h = at
                out = bank_for(at)
                w = arrived(("in", c)).rearrange("p (k n) -> p k n", k=KD)
                halves = out[:, :].rearrange("p (a t) -> p a t", a=2)
                if c in (2, 3, 0, 6) or at == ("in", 5, 1):
                    for a in range(2):
                        ct = 2 + a if c == 5 else 2 * h + a
                        for k in range(KD):
                            ins = mm(halves[:, a], w[:, k, ct * P:(ct + 1) * P], h_t[:, k, :], start=k == 0, stop=k == KD - 1)
                elif c == 5:
                    for g in range(G):
                        for k in range(KD):
                            ins = mm(halves[:, g], h_t[:, k, tok(g)], w[:, k, 0:FW], start=k == 0, stop=k == KD - 1)
                else:
                    for k in range(KD):
                        ins = mm(out[:, :], h_t[:, k, tok(h)], w[:, k, :], start=k == 0, stop=k == KD - 1)
                ins.then_inc(product_ready, 1)
                if h == 1:
                    nc.tensor.drain().then_inc(chunk_used, 1)

            def scan_scores(s):
                d, g, n = STEPS[s]
                out = scratch_for(("step", s))
                if d is None:
                    pe.wait_ge(key_sum_ready, g + 1)
                else:
                    pe.wait_ge(q_ready, s + 1)
                    pe.wait_ge(k_ready, s + 1)
                for h in range(HEADS):
                    query = q_t[:, h, tok(g)] if d is None else lev_q[:, s % 2, h, :]
                    ins = mm(out[:, h * P:(h + 1) * P], lev_k[:, s % 2, h, :], query, start=True, stop=True)
                ins.then_inc(scratch_ready, 1)

            def stage(name):
                if name == "scan output":
                    for g in range(G):
                        out = scratch_for(("four1", g))
                        for ct in range(2):
                            ins = mm(out[:, ct * 2 * P:(ct + 1) * 2 * P], four[:, g, ct * P:(ct + 1) * P], dft[:, 0:2 * P], start=True, stop=True)
                        ins.then_inc(scratch_ready, 1)
                    for g in range(G):
                        pe.wait_ge(*read_out(("step", 2 * G * len(LEVELS) + g)))
                        if g == 1:
                            pe.wait_ge(start_q_ready, 2)
                        for h in range(HEADS):
                            out = o_bank[g][:, h * DK:(h + 1) * DK]
                            v = value[:, g, h * DK:(h + 1) * DK]
                            ins = mm(out, scores[:, g, h, :], v, start=True, stop=g == 0)
                            if g == 1:
                                for d in range(2):
                                    ins = mm(out, lev_q[:, d, h, :], state_in[:, d, h, :], start=False, stop=d == 1)
                        ins.then_inc(o_ready, 1)
                elif name == "final keys":
                    for d in range(2):
                        pe.wait_ge(end_key_ready, d + 1)
                        turn_tiles(("ends", d), [kd_sb[:, d, h, :] for h in range(HEADS)])
                elif name == "final states":
                    for d in range(2):
                        pe.wait_ge(*read_out(("ends", d)))
                        out = scratch_for(("state", d))
                        for h in range(HEADS):
                            ins = mm(out[:, h * DK:(h + 1) * DK], kd_t[:, d, h, :], value[:, 0, h * DK:(h + 1) * DK], start=True, stop=True)
                        ins.then_inc(scratch_ready, 1)
                elif name == "fourier":
                    for g in range(G):
                        pe.wait_ge(*read_out(("four1", g)))
                    out = scratch_for(("four2",))
                    for ct in range(2):
                        for g in range(G):
                            at = out[:, ct * TOK + g * P:ct * TOK + (g + 1) * P]
                            mm(at, dft[:, 2 * P:3 * P], four_f[:, g, ct, 0:P], start=True, stop=False)
                            ins = mm(at, dft[:, 3 * P:4 * P], four_f[:, g, ct, P:2 * P], start=False, stop=True)
                    ins.then_inc(scratch_ready, 1)
                else:
                    for g in range(G):
                        pe.wait_ge(a_ready, g + 1)
                        turn_tiles(("a", g), [out_gate[:, g, h * DK:(h + 1) * DK] for h in range(HEADS)])

            pe.wait_ge(cond_ready, 1)

            def sum_parts(c):
                pe.wait_ge(*evacuated(("ada", c)))
                out = scratch_for(("mod", c))
                for ct in range(BANK // P):
                    ins = mm(out[:, ct * G:(ct + 1) * G], mod_part[:, c % 2, ct * P:(ct + 1) * P], con("row_sum"), start=True, stop=True)
                ins.then_inc(scratch_ready, 1)

            pe.wait_ge(cond_pad_ready, 1)
            for c in ADA_EARLY:
                modulation(c, cond_pad, COLS)
                if c == 1:
                    pe.wait_ge(cst_in, 16)
                if c:
                    sum_parts(c - 1)
            sum_parts(ADA_EARLY[-1])
            pe.wait_ge(cst_in, 16)
            for g in range(G):
                pe.wait_ge(norm_ready, g + 1)
                for a in range(2):
                    turn_tiles(("h", g, a), [h_tok[:, g, k * P:(k + 1) * P] for k in range(4 * a, 4 * a + 4)])
            for g in range(G):
                for a in range(2):
                    pe.wait_ge(*read_out(("h", g, a)))
            for what, at in schedule(False):
                if what == "stage":
                    stage(at)
                elif what == "step":
                    scan_scores(at)
                elif at[0] == "ada":
                    modulation(at[1])
                else:
                    w_in_product(at)

            pe.wait_ge(*read_out(("four2",)))
            pe.wait_ge(conv_ready, 1)
            w_a = arrived(("proj_hgrn", 0)).rearrange("p (k n) -> p k n", k=HEADS)
            w_fc = arrived(("proj_fc", 0)).rearrange("p (b k n) -> p b k n", b=2, k=2)
            for g in range(G):
                for h in range(2):
                    cols = slice(h * BANK, (h + 1) * BANK)
                    for b in BRANCH_ORDER:
                        if b == 0:
                            pe.wait_ge(*read_out(("a", g)))
                        out = bank_for(("proj", g, h, b))
                        left = (a_t, f_t, c_t)[b]
                        right = (w_a, w_fc[:, 0], w_fc[:, 1])[b]
                        n_k = HEADS if b == 0 else 2
                        for k in range(n_k):
                            ins = mm(out[:, :], left[:, k, tok(g)], right[:, k, cols], start=k == 0, stop=k == n_k - 1)
                        ins.then_inc(product_ready, 1)
            nc.tensor.drain().then_inc(chunk_used, 2)
            for g in range(G):
                for a in range(2):
                    pe.wait_ge(merged_ready, 2 * g + a + 1)
                    turn_tiles(("merged", g, a), [merged[:, g, k * P:(k + 1) * P] for k in range(4 * a, 4 * a + 4)])
            for g in range(G):
                for a in range(2):
                    pe.wait_ge(*read_out(("merged", g, a)))
            for h in range(2):
                w = arrived(("out", h)).rearrange("p (k n) -> p k n", k=KD)
                for g in range(G):
                    out = bank_for(("out", h, g))
                    for k in range(KD):
                        ins = mm(out[:, :], h_t[:, k, tok(g)], w[:, k, :], start=k == 0, stop=k == KD - 1)
                    ins.then_inc(product_ready, 1)
                nc.tensor.drain().then_inc(chunk_used, 1)
            nc.tensor.drain().then_inc(mixer_done, 1)
            for c in ADA_LAST:
                modulation(c)

            def shared_up(f, g):
                for b in range(2):
                    for k in range(KD):
                        ins = mm(rotating(("shared", f))[:, b * TOK + g * P:b * TOK + (g + 1) * P], w_up[:, b, k, f * P:(f + 1) * P],
                                 h_t[:, k, tok(g)], start=k == 0, stop=k == KD - 1)
                if g == G - 1:
                    ins.then_inc(product_ready, 1)

            for g in range(G):
                pe.wait_ge(norm_ready, G + g + 1)
                for a in range(2):
                    turn_tiles(("h2", g, a), [h2_tok[:, g, :].rearrange("p (q k) -> p k q", k=KD)[:, k] for k in range(4 * a, 4 * a + 4)])
                for a in range(2):
                    pe.wait_ge(*read_out(("h2", g, a)))
                if g == 0:
                    bank_for(("shared", 0))
                    w_up = arrived(("shared_up", 0)).rearrange("p (b k n) -> p b k n", b=2, k=KD)
                    shared_up(0, 0)
                    pe.wait_ge(router_in, 32)
                    pe.wait_ge(a_ready, 1)
                for k in range(KD):
                    ins = mm(scratch(("logits",))[:, g * N_EXP:(g + 1) * N_EXP], h_t[:, k, tok(g)], w_rt[:, k, :], start=k == 0, stop=k == KD - 1)
            ins.then_inc(scratch_ready, 1)
            pe.wait_ge(chosen_ready, 1)
            out = scratch_for(("place",))
            mm(out[:, 0:N_EXP], before, chosen[:, 0, :], start=True, stop=True)
            mm(out[:, N_EXP:2 * N_EXP], ones, chosen[:, 0, :], start=True, stop=False)
            mm(out[:, N_EXP:2 * N_EXP], before, chosen[:, 1, :], start=False, stop=True).then_inc(scratch_ready, 1)
            out = scratch_for(("count",))
            for g in range(G):
                ins = mm(out[0:N_EXP, 0:1], chosen[:, g, :], ones[:, 0:1], start=g == 0, stop=g == G - 1)
            ins.then_inc(scratch_ready, 1)
            pe.wait_ge(counted, 1)
            out = scratch_for(("before",))
            mm(out[0:N_EXP, 0:1], before[0:N_EXP, 0:N_EXP], n_chunks[0:N_EXP, :], start=True, stop=True)
            mm(out[0:1, 1:2], n_chunks[0:N_EXP, :], ones[0:N_EXP, 0:1], start=True, stop=True).then_inc(scratch_ready, 1)
            out = scratch_for(("rows",))
            for i, t in enumerate([place[:, 0, :], place[:, 1, :], weight[:, 0, :], weight[:, 1, :]]):
                ins = nc.tensor.transpose(out[0:N_EXP, i * P:(i + 1) * P], t, ident)
            ins.then_inc(scratch_ready, 1)
            shared_up(0, 1)
            pe.wait_ge(listed, MAX_CHUNKS)
            out = scratch_for(("items",))
            mm(out[0:1, 0:MAX_ITEMS], con("part_no")[0:N_EXP, :], of_item[:, :], start=True, stop=True)
            mm(out[:, P:P + MAX_ITEMS], ones[0:N_EXP, :], at_item[:, :], start=True, stop=True).then_inc(scratch_ready, 1)
            pe.wait_ge(*read_out(("rows",)))
            out = scratch_for(("item_rows",))
            for a in range(2):
                for g in range(G):
                    i = (a * G + g) * MAX_ITEMS
                    ins = mm(out[:, i:i + MAX_ITEMS], rows_t[:, a, g, :], of_item[:, :], start=True, stop=True)
            ins.then_inc(scratch_ready, 1)
            for g in range(G):
                shared_up(1, g)
            nc.tensor.drain().then_inc(chunk_used, 1)
            for s in mod_stored:
                pe.wait_ge(s, 16 * len(ADA_ROWS) // 2)
            pe.wait_ge(split_ready, G)
            pe.wait_ge(h_lo_ready, G)
            nc.tensor.drain().then_inc(split_free, 1)
            for f in range(2):
                pe.wait_ge(*evacuated(("shared", f)))
            for g in range(G):
                pe.wait_ge(a_ready, g + 1)
            w = arrived(("shared_down", 0))[:, 0:2 * D].rearrange("p (k n) -> p k n", k=2)
            for g in range(G):
                for h in range(2):
                    for f in range(2):
                        ins = mm(acc_bank[2 * g + h][:, :], hid_sh[:, f, tok(g)], w[:, f, h * BANK:(h + 1) * BANK], start=f == 0, stop=f == 1)
            nc.tensor.drain().then_inc(chunk_used, 1)
            pe.wait_ge(*read_out(("items",)))
            pe.wait_ge(*read_out(("item_rows",)))

            def gather(j):
                n = j * ITEMS_PER_TURN
                pe.wait_ge(pick_ready, val(j + 1))
                for u in range(KD + 1):
                    out = gather_bank[u]
                    if u == 0:
                        need(gu_sum_ready, n)
                        need(gu_lo_ready, n)
                    elif u == 1:
                        need(put_back_ready, n)
                        need(hid_hi_ready, n - 1)
                        need(hid_lo_ready, n - 1)
                    elif u in (2, 3):
                        need(y_hi_ready, 2 * (n - 1))
                        need(y_lo_ready, 2 * (n - 1))
                    elif u == 4:
                        pe.wait_ge(slot_gate_ready, val(j + 1))
                    else:
                        pe.wait_ge(*tile_out(j, u - 5 if u < KD else 4))
                    if u == 0:
                        for q in range(ITEMS_PER_TURN):
                            for g in range(G):
                                ins = mm(out[0:SLOTS, q:q + 1], pick[:, g, q, 0:SLOTS].bitcast(F32), gate4[:, g, q:q + 1], start=g == 0, stop=g == G - 1)
                    else:
                        by_item = out[:, :].rearrange("p (q b s) -> p q b s", q=ITEMS_PER_TURN, b=2)
                        for b, part in enumerate((h_hi, h_lo)):
                            for g in range(G):
                                ins = mm(by_item[:, :, b, :], part[:, g, u - 1, :], pick[:, g, :, 0:SLOTS], start=g == 0, stop=g == G - 1)
                    ins.then_inc(gathered, 1)

            def up(j, c, a, q):
                s = c % N_SPLIT
                if q == 0:
                    for k in (2, 3) if a == 0 else (5, 7):
                        pe.wait_ge(*tile_out(j, k))
                pe.wait_ge(low_up_ready, val(2 * (j * ITEMS_PER_TURN + q) + a + 1))
                for k in range(KD // 2):
                    for b, w in enumerate((w_hi, w_lo)):
                        ins = mm(gu_bank[:, :], x_g[:, a * KD // 2 + k, q, :], w[:, s, k * BANK:(k + 1) * BANK],
                                 start=a == k == b == 0, stop=a == b == 1 and k == KD // 2 - 1)
                ins.then_inc(piece_used, 1)

            def turn_over(n, hidden, q):
                if hidden:
                    pe.wait_ge(hid_ready, val(n))
                need(put_back_ready, n)
                need(hid_hi_ready, n - 1)
                need(hid_lo_ready, n - 1)
                if q is None:
                    scatter(n - 2, ITEMS_PER_TURN - 2)
                else:
                    for g in range(G):
                        ins = nc.tensor.transpose(turn_bank[:, (1 + g) * P:(2 + g) * P], pick[:, g, q, :].bitcast(F32), ident)
                if hidden:
                    for f in range(2):
                        ins = nc.tensor.transpose(turn_bank[:, f * SLOTS:(f + 1) * SLOTS], hid[:, f::2], ident[0:SLOTS, 0:SLOTS])
                ins.then_inc(turned, 1)

            def scatter(m, q):
                pe.wait_ge(put_back_ready, val(m + 1))
                pe.wait_ge(y_lo_ready, val(2 * m + 2))
                for g in range(G):
                    for h in range(2):
                        for y in (y_hi, y_lo):
                            ins = mm(acc_bank[2 * g + h][:, :], put_back[:, q, g, :], y[:, h, :], start=False, stop=True, skip_group_check=True)
                ins.then_inc(scattered, 1)

            def down(c, m):
                s = c % N_SPLIT
                pe.wait_ge(low_down_ready, val(m + 1))
                pe.wait_ge(hid_lo_ready, val(m + 1))
                need(y_lo_ready, 2 * m)
                for h in range(2):
                    for f in range(2):
                        for b, w in enumerate((w_hi, w_lo)):
                            ins = mm(y_bank[h][:, :], hid_t[:, f, :], w[:, s, f * D + h * BANK:f * D + (h + 1) * BANK],
                                     start=f == b == 0, stop=f == b == 1)
                    ins.then_inc(piece_used if h else y0_ready, 1)

            def turn(j, first):
                gather(j)
                for q in range(ITEMS_PER_TURN):
                    n = j * ITEMS_PER_TURN + q
                    start = first and q == 0
                    need(gu_sum_ready, n)
                    up(j, 3 * q - 1 + start, 0, q)
                    up(j, 3 * q + start, 1, q)
                    turn_over(n, not start, q)
                    if not (first and q < 2):
                        scatter(n - 2, (q - 2) % ITEMS_PER_TURN)
                    if not start:
                        down(3 * q + 1, n - 1)

            more_turns = turns_after_first(pe)
            turn(0, True)
            with pe.Fori(0, more_turns) as t:
                turn(Count(t, 1, 1), False)
            turns = Count(more_turns, 1, 1)
            n_items = turns * ITEMS_PER_TURN
            turn_over(n_items, True, None)
            down(-1, n_items - 1)
            scatter(n_items - 1, ITEMS_PER_TURN - 1)
            nc.tensor.drain().then_inc(moe_done, 1)


_INS = ['x_prompt', 'x_sample', 'c', 'state_hgrn', 'c_ctx', 'w_ada', 'b_ada', 'w_in', 'b_gate', 'hgrn_lb', 'hgrn_norm',
        'conv_w', 'w_proj_hgrn', 'w_proj_fourier', 'w_proj_conv', 'w_out', 'ln1_g', 'ln1_b', 'ln2_g', 'ln2_b',
        'w_router', 'b_router', 'w_exp_gate', 'w_exp_up', 'w_exp_down', 'w_sh_gate', 'w_sh_up', 'w_sh_down']
_OUTS = [("y_prompt_out", (1, P, D)), ("y_sample_out", (1, P, D)), ("state_out_dram", (1, 1, 2, HEADS, DK, DK))]


def kernel(**inputs):
    import concourse.bacc as bacc
    from concourse.bass_utils import run_bass_kernel_spmd

    nc = bacc.Bacc("TRN2", target_bir_lowering=False, num_devices=1)
    arrays = {f"in_{name}": np.ascontiguousarray(inputs[name]) for name in _INS}
    arrays |= {"shape_table": CST, "shape_masks": MASKS, "shape_pos": POS}
    args = [nc.dram_tensor(n, a.shape, mybir.dt.from_np(a.dtype), kind="ExternalInput").ap() for n, a in arrays.items()]
    args += [nc.dram_tensor(n, shape, F32, kind="ExternalOutput").ap() for n, shape in _OUTS]
    hybrid_layer(nc, *args)
    r = run_bass_kernel_spmd(nc, [arrays], core_ids=[0])
    return tuple(r.results[0][n] for n, _ in _OUTS)
```
